# Optimizing a Trainium2 kernel written in Bass

```python
import math, functools
import jax, jax.numpy as jnp
from jax import lax
import numpy as np

D_MODEL = 1024
BATCH = 1
SEQ = 512
DEPTH = 1
DEC_BATCH = 8
DEC_SEQ = 4
PAST_LEN = 1024
PAGE_SIZE = 128

D_A = D_MODEL // 2
G_A = 4
C_G = D_A // G_A
CHUNK = 128
HEAD_DIM = 64
H_G = 8
GROUPS = ((128, 1), (512, 4), (2048, 16))
N_GROUPS = 3
N_HEADS_B = H_G * N_GROUPS
D_QKV = N_HEADS_B * HEAD_DIM
D_B_OUT = H_G * HEAD_DIM
N_KEYS = 129
SUB_BLOCK = 128
ROT_DIM = HEAD_DIM // 4
ROPE_THETA = 500000.0
D_FF = 4 * D_MODEL
D_PLE = 256
D_IN = 2 * D_A + 3 * D_QKV + 2 * D_MODEL
EPS = 1e-6
NEG = -1e30

kernel_name = "gated_gmlp_dilated_attn_decoder_step"

def _rmsnorm(x, g):
    xf = x.astype(jnp.float32)
    y = xf * lax.rsqrt(jnp.mean(xf * xf, axis=-1, keepdims=True) + EPS) * g.astype(jnp.float32)
    return y.astype(x.dtype)

def _rotary(x, pos):
    half = ROT_DIM // 2
    inv = ROPE_THETA ** (-jnp.arange(half, dtype=jnp.float32) * 2.0 / ROT_DIM)
    ang = pos.astype(jnp.float32)[:, None] * inv[None, :]
    cos = jnp.cos(ang)[:, None, :]
    sin = jnp.sin(ang)[:, None, :]
    x1 = x[..., :half].astype(jnp.float32)
    x2 = x[..., half:ROT_DIM].astype(jnp.float32)
    rot = jnp.concatenate([x1 * cos - x2 * sin, x2 * cos + x1 * sin], axis=-1).astype(x.dtype)
    return jnp.concatenate([rot, x[..., ROT_DIM:]], axis=-1)

def _chunk_mix_prompt(u, v, w_s, b_s):
    B, S, _ = u.shape
    ws = jnp.tril(w_s.astype(jnp.float32))
    vc = v.astype(jnp.float32).reshape(B, S // CHUNK, CHUNK, G_A, C_G)
    mix = jnp.einsum('gts,bcsgd->bctgd', ws, vc) + b_s.astype(jnp.float32).T[None, None, :, :, None]
    return (u.astype(jnp.float32) * mix.reshape(B, S, D_A)).astype(u.dtype)

def _chunk_mix_sample(u, v, w_s, b_s):
    B, T, _ = u.shape
    ws = jnp.tril(w_s.astype(jnp.float32))[:, :T, :T]
    vc = v.astype(jnp.float32).reshape(B, T, G_A, C_G)
    mix = jnp.einsum('gts,bsgd->btgd', ws, vc) + b_s.astype(jnp.float32)[:, :T].T[None, :, :, None]
    return (u.astype(jnp.float32) * mix.reshape(B, T, D_A)).astype(u.dtype)

def _dilated_group_prompt(q, k, v, d):
    B, S, H, Dh = q.shape
    span = SUB_BLOCK * d
    L = -(-S // span) * span
    nb = L // span

    def to_blocks(t):
        t = jnp.pad(t.astype(jnp.float32), ((0, 0), (0, L - S), (0, 0), (0, 0)))
        t = t.reshape(B, L // d, d, H, Dh).transpose(0, 2, 1, 3, 4)
        return t.reshape(B, d, nb, SUB_BLOCK, H, Dh)

    def with_prev(t):
        prev = jnp.pad(t[:, :, :-1], ((0, 0), (0, 0), (1, 0), (0, 0), (0, 0), (0, 0)))
        return jnp.concatenate([prev, t], axis=3)

    qb = to_blocks(q)
    kk = with_prev(to_blocks(k))
    vv = with_prev(to_blocks(v))
    s = jnp.einsum('brnqhd,brnkhd->brnhqk', qb, kk) / math.sqrt(Dh)
    i = jnp.arange(SUB_BLOCK)[:, None]
    j = jnp.arange(2 * SUB_BLOCK)[None, :]
    rel = SUB_BLOCK + i - j
    band = (rel >= 0) & (rel <= N_KEYS - 1)
    exists = (jnp.arange(nb)[:, None, None] > 0) | (j >= SUB_BLOCK)[None]
    mask = (band[None] & exists)[None, None, :, None]
    s = jnp.where(mask, s, NEG)
    m = jnp.max(s, axis=-1, keepdims=True)
    e = jnp.exp(s - m)
    den = jnp.sum(e, axis=-1, keepdims=True)
    o = jnp.einsum('brnhqk,brnkhd->brnhqd', e, vv) / den
    lse = (m + jnp.log(den))[..., 0]
    o = o.transpose(0, 1, 2, 4, 3, 5).reshape(B, d, L // d, H, Dh)
    o = o.transpose(0, 2, 1, 3, 4).reshape(B, L, H, Dh)[:, :S]
    lse = lse.transpose(0, 1, 2, 4, 3).reshape(B, d, L // d, H)
    lse = lse.transpose(0, 2, 1, 3).reshape(B, L, H)[:, :S]
    return o, lse

def _dilated_group_sample(q, k, v, kv_buf, d):
    T = q.shape[1]
    Wb = kv_buf.shape[2]
    kk = jnp.concatenate([kv_buf[:, 0], k.astype(kv_buf.dtype)], axis=1)
    vv = jnp.concatenate([kv_buf[:, 1], v.astype(kv_buf.dtype)], axis=1)
    idx = Wb + jnp.arange(T)[:, None] - jnp.arange(N_KEYS)[None, :] * d
    valid = idx >= 0
    idx = jnp.maximum(idx, 0)
    kg = kk[:, idx].astype(jnp.float32)
    vg = vv[:, idx].astype(jnp.float32)
    s = jnp.einsum('bthd,btjhd->bhtj', q.astype(jnp.float32), kg) / math.sqrt(q.shape[-1])
    s = jnp.where(valid[None, None], s, NEG)
    m = jnp.max(s, axis=-1, keepdims=True)
    e = jnp.exp(s - m)
    den = jnp.sum(e, axis=-1, keepdims=True)
    o = jnp.einsum('bhtj,btjhd->bhtd', e, vg) / den
    lse = (m + jnp.log(den))[..., 0]
    new_buf = jnp.stack([kk[:, -Wb:], vv[:, -Wb:]], axis=1)
    return o.transpose(0, 2, 1, 3), lse.transpose(0, 2, 1), new_buf

def _combine(outs, lses, dtype):
    w = jax.nn.softmax(jnp.stack(lses, axis=0), axis=0)[..., None]
    o = jnp.sum(w * jnp.stack(outs, axis=0), axis=0)
    return o.reshape(*o.shape[:-2], D_B_OUT).astype(dtype)

def _dilated_prompt(q, k, v):
    S = q.shape[1]
    outs, lses, states = [], [], []
    for gi, (win, dil) in enumerate(GROUPS):
        sl = slice(gi * H_G, (gi + 1) * H_G)
        o, lse = _dilated_group_prompt(q[:, :, sl], k[:, :, sl], v[:, :, sl], dil)
        outs.append(o)
        lses.append(lse)
        wb = min(win, S)
        states.append(jnp.stack([k[:, S - wb:, sl], v[:, S - wb:, sl]], axis=1))
    return _combine(outs, lses, q.dtype), states

def _dilated_sample(q, k, v, bufs):
    outs, lses, states = [], [], []
    for gi, (win, dil) in enumerate(GROUPS):
        sl = slice(gi * H_G, (gi + 1) * H_G)
        o, lse, nb = _dilated_group_sample(q[:, :, sl], k[:, :, sl], v[:, :, sl], bufs[gi], dil)
        outs.append(o)
        lses.append(lse)
        states.append(nb)
    return _combine(outs, lses, q.dtype), states

def _layer(x, pe, pos, g_mix, w_in, g_v, w_s, b_s, g_q, g_k, w_oa, w_ob, w_o,
           g_ffn, w_ff1, w_ff2, g_ple, w_ple_gate, w_ple_proj, mix_a, mix_b):
    lead = x.shape[:-1]
    h = _rmsnorm(x, g_mix)
    z = h @ w_in
    cuts = [D_A, 2 * D_A, 2 * D_A + D_QKV, 2 * D_A + 2 * D_QKV, 2 * D_A + 3 * D_QKV,
            2 * D_A + 3 * D_QKV + D_MODEL]
    u, va, q, k, v, gate_a, gate_b = jnp.split(z, cuts, axis=-1)
    u = jax.nn.gelu(u)
    va = _rmsnorm(jax.nn.gelu(va), g_v)
    a = mix_a(u, va, w_s, b_s)
    q = _rotary(_rmsnorm(q.reshape(*lead, N_HEADS_B, HEAD_DIM), g_q), pos)
    k = _rotary(_rmsnorm(k.reshape(*lead, N_HEADS_B, HEAD_DIM), g_k), pos)
    v = v.reshape(*lead, N_HEADS_B, HEAD_DIM)
    b, kv_states = mix_b(q, k, v)
    merged = jax.nn.sigmoid(gate_a) * (a @ w_oa) + jax.nn.sigmoid(gate_b) * (b @ w_ob)
    x = x + merged @ w_o
    h2 = _rmsnorm(x, g_ffn)
    x = x + jnp.square(jax.nn.relu(h2 @ w_ff1)) @ w_ff2
    gate = jax.nn.sigmoid(_rmsnorm(x, g_ple) @ w_ple_gate)
    x = x + gate * (pe @ w_ple_proj)
    return x, kv_states, va

def setup_inputs(seed: int = 0) -> dict:
    key = jax.random.key(seed)
    ks = jax.random.split(key, 32)
    f32 = jnp.float32

    def nrm(k, shape, scale=1.0):
        return jax.random.normal(k, shape, f32) * scale

    def gain(k, shape):
        return 1.0 + 0.05 * jax.random.normal(k, shape, f32)

    out = {
        "x_prompt": nrm(ks[0], (BATCH, SEQ, D_MODEL)),
        "x_sample": nrm(ks[1], (DEC_BATCH, DEC_SEQ, D_MODEL)),
        "p_prompt": nrm(ks[2], (DEPTH, BATCH, SEQ, D_PLE)),
        "p_sample": nrm(ks[3], (DEPTH, DEC_BATCH, DEC_SEQ, D_PLE)),
        "cache_kv_w128": nrm(ks[4], (DEPTH, DEC_BATCH, 2, min(GROUPS[0][0], PAST_LEN), H_G, HEAD_DIM)),
        "cache_kv_w512": nrm(ks[5], (DEPTH, DEC_BATCH, 2, min(GROUPS[1][0], PAST_LEN), H_G, HEAD_DIM)),
        "cache_kv_w2048": nrm(ks[6], (DEPTH, DEC_BATCH, 2, min(GROUPS[2][0], PAST_LEN), H_G, HEAD_DIM)),
        "g_mix": gain(ks[7], (DEPTH, D_MODEL)),
        "w_in": nrm(ks[8], (DEPTH, D_MODEL, D_IN), D_MODEL ** -0.5),
        "g_v": gain(ks[9], (DEPTH, D_A)),
        "w_s": nrm(ks[10], (DEPTH, G_A, CHUNK, CHUNK), CHUNK ** -0.5),
        "b_s": 1.0 + 0.1 * nrm(ks[11], (DEPTH, G_A, CHUNK)),
        "g_q": gain(ks[12], (DEPTH, HEAD_DIM)),
        "g_k": gain(ks[13], (DEPTH, HEAD_DIM)),
        "w_oa": nrm(ks[14], (DEPTH, D_A, D_MODEL), D_A ** -0.5),
        "w_ob": nrm(ks[15], (DEPTH, D_B_OUT, D_MODEL), D_B_OUT ** -0.5),
        "w_o": nrm(ks[16], (DEPTH, D_MODEL, D_MODEL), D_MODEL ** -0.5),
        "g_ffn": gain(ks[17], (DEPTH, D_MODEL)),
        "w_ff1": nrm(ks[18], (DEPTH, D_MODEL, D_FF), D_MODEL ** -0.5),
        "w_ff2": nrm(ks[19], (DEPTH, D_FF, D_MODEL), D_FF ** -0.5),
        "g_ple": gain(ks[20], (DEPTH, D_MODEL)),
        "w_ple_gate": nrm(ks[21], (DEPTH, D_MODEL, D_MODEL), D_MODEL ** -0.5),
        "w_ple_proj": nrm(ks[22], (DEPTH, D_PLE, D_MODEL), D_PLE ** -0.5),
    }
    return out

def reference(x_prompt, x_sample, p_prompt, p_sample, cache_kv_w128, cache_kv_w512, cache_kv_w2048,
              g_mix, w_in, g_v, w_s, b_s, g_q, g_k, w_oa, w_ob, w_o,
              g_ffn, w_ff1, w_ff2, g_ple, w_ple_gate, w_ple_proj):
    S = x_prompt.shape[1]
    T = x_sample.shape[1]
    pos_p = jnp.arange(S, dtype=jnp.int32)
    pos_s = PAST_LEN + jnp.arange(T, dtype=jnp.int32)
    xp, xs = x_prompt, x_sample
    kvp = ([], [], [])
    kvs = ([], [], [])
    cvp, cvs = [], []
    for l in range(DEPTH):
        lw = (g_mix[l], w_in[l], g_v[l], w_s[l], b_s[l], g_q[l], g_k[l], w_oa[l], w_ob[l], w_o[l],
              g_ffn[l], w_ff1[l], w_ff2[l], g_ple[l], w_ple_gate[l], w_ple_proj[l])
        xp, st_p, va_p = _layer(xp, p_prompt[l], pos_p, *lw,
                                mix_a=_chunk_mix_prompt, mix_b=_dilated_prompt)
        bufs = (cache_kv_w128[l], cache_kv_w512[l], cache_kv_w2048[l])
        xs, st_s, va_s = _layer(xs, p_sample[l], pos_s, *lw,
                                mix_a=_chunk_mix_sample,
                                mix_b=functools.partial(_dilated_sample, bufs=bufs))
        for gi in range(N_GROUPS):
            kvp[gi].append(st_p[gi])
            kvs[gi].append(st_s[gi])
        cvp.append(va_p[:, S - CHUNK:])
        cvs.append(va_s)
    kv128_prompt = jnp.stack(kvp[0], axis=0)
    kv512_prompt = jnp.stack(kvp[1], axis=0)
    kv2048_prompt = jnp.stack(kvp[2], axis=0)
    kv128_sample = jnp.stack(kvs[0], axis=0)
    kv512_sample = jnp.stack(kvs[1], axis=0)
    kv2048_sample = jnp.stack(kvs[2], axis=0)
    chunk_v_prompt = jnp.stack(cvp, axis=0)
    chunk_v_sample = jnp.stack(cvs, axis=0)
    return (xp, xs, kv128_prompt, kv512_prompt, kv2048_prompt,
            kv128_sample, kv512_sample, kv2048_sample, chunk_v_prompt, chunk_v_sample)


_drawn_inputs = setup_inputs


def setup_inputs(seed=0):
    import zlib

    import numpy as np

    out = dict(_drawn_inputs(seed))
    spreads = {}
    factors = {'g_q': 8.0, 'g_ple': 23.658}
    for name, (base, spread) in spreads.items():
        noise = np.random.default_rng([zlib.crc32(name.encode()), seed]).standard_normal(out[name].shape)
        drawn = base * np.exp(spread * noise) if base else spread * noise
        out[name] = __import__('jax').numpy.asarray(drawn.astype(out[name].dtype))
    for name, factor in factors.items():
        out[name] = (out[name] * factor).astype(out[name].dtype)
    return out
```

```python
import numpy as np
import concourse.bass as bass
from concourse import mybir
from contextlib import ExitStack

F32, F32R, BF16 = mybir.dt.float32, mybir.dt.float32r, mybir.dt.bfloat16
ALU, ACT, AX = mybir.AluOpType, mybir.ActivationFunctionType, mybir.AxisListType

D, SEQ, NB, T = 1024, 512, 8, 4
NS = NB * T
NT = SEQ + NS
HALF = NT // 2
H, HD, NG = 8, 64, 3
WIN = (128, 512, 1024)
QKV = H * NG * HD
DA, DPLE, DFF = 512, 256, 4096
KD = D // 128
HP = 2 * KD + 1
EPS, SCALE = 1e-6, HD ** -0.5
GELU_A, GELU_B = 0.044715, 0.7978845608028654

PANELS = []
for _g in range(NG):
    for _kind in ("k", "q", "v"):
        PANELS += [(_kind, _g, 0), (_kind, _g, 1)]
PANELS += [("va", 0, 0), ("va", 0, 1), ("u", 0, 0), ("u", 0, 1)]
PANELS += [("ga", 0, 0), ("ga", 0, 1), ("oa", 0, 0), ("ga", 0, 2), ("ga", 0, 3), ("oa", 0, 1)]
PANELS += [("gb", 0, i) for i in range(4)] + [("ob", 0, 0), ("ob", 0, 1)]
PANELS += [("wo", 0, i) for i in range(4)] + [("pj", 0, 0)]
P_FF = len(PANELS)
NATURAL = ("k", "q", "v", "va")
COLS = {"oa": 512, "ob": 512, "pj": 1024}
UNITS = []
for _p, (_kind, _g, _i) in enumerate(PANELS):
    _n = 3 if _kind in NATURAL else COLS.get(_kind, 256) // 128
    UNITS += [(_p, _kind, _g, _i, _s) for _s in range(_n)]
U_FF = len(UNITS)
NFF = 4
FF_PANELS, FF_UNITS = 8, 16
P_PG, U_PG = P_FF + NFF * FF_PANELS, U_FF + NFF * FF_UNITS
STAGED = [k not in ("v", "ga", "gb", "pj") for (_, k, _, _, _) in UNITS]
UNIT = {}
for _u, (_p, _kind, _g, _i, _s) in enumerate(UNITS):
    UNIT[_kind, _i * (COLS.get(_kind, 256) // 128) + _s if _kind not in NATURAL else (_g, _i, _s)] = _u
SQ_KINDS = ("k", "q", "va", "u")


def sq_count(u):
    return sum(1 for x in UNITS[:u + 1] if x[1] in SQ_KINDS)


GELU = [u for u in range(U_FF) if UNITS[u][1] in ("va", "u")]


def zc(u):
    return sum(STAGED[:u + 1]) + max(0, u + 1 - U_FF)


def panel_end(p):
    if p < P_FF:
        return max(u for u in range(U_FF) if UNITS[u][0] == p) + 1
    return U_FF + 2 * (p - P_FF + 1)


def kqn(u):
    return sum(1 for x in UNITS[:u] if x[1] in ("k", "q"))


def stores_keys(u):
    return UNITS[u][1] == "k" and not (UNITS[u][2] == 0 and UNITS[u][4] == 0)


PIECES = [(0, h, b) for h in range(H) for b in range(2)] + [(1, h, 0) for h in range(H)] + [(2, h, 0) for h in range(H)]
PIECE_SLOT = [18 + j for j in range(16)] + [36 + j for j in range(8)] + [54 + j for j in range(8)]
S_AT = {s: j for j, s in enumerate(PIECE_SLOT)}
BUFS = [(0, 0), (0, 4)] + [(1, b) for b in range(8)] + [(2, b) for b in range(0, 8, 2)]
KT_AT = {}
for _n in range(8):
    KT_AT[18 + _n] = (0, _n, 0, 1, _n // 4, _n % 4)
for _n in range(16):
    KT_AT[36 + _n] = (1, _n // 2, 2 * (_n % 2), 2, 2 + _n // 2, 2 * (_n % 2))
for _n in range(8):
    KT_AT[52 + _n] = (2, _n, 0, 2, 10 + _n // 2, 2 * (_n % 2))
NBUF = len(BUFS)
V_SLOT0 = 68
SLOTS = U_FF
COPY_AT = list(range(0, 96, 3))

TJOBS = {}
TINDEX = {}


def _plan_tjobs():
    n = 0
    order = [(-1, ("h", k)) for k in range(KD)] + [(-1, ("hs",))]
    for s in range(SLOTS):
        if s >= 2 and UNITS[s - 2][1] in ("k", "q"):
            order.append((s, ("qk", s - 2)))
        if s - 1 in S_AT:
            order.append((s, ("pt", S_AT[s - 1])))
        if s == 50:
            order.append((s, ("ws",)))
        if s in KT_AT:
            order += [(s, ("kt", s, x)) for x in range(KT_AT[s][3])]
        if s == 63:
            order += [(s, ("ss", 0)), (s, ("ss", 1))]
        if s == 65:
            order += [(s, ("mix", g)) for g in range(4)] + [(s, ("mixs",))]
        if s == 67:
            order += [(s, (x, hf)) for hf in range(2) for x in ("pa", "pb")]
        if s == 72:
            order += [(s, ("bt", c)) for c in range(4)]
        if 88 <= s < 96:
            order.append((s, ("x", s - 88)))
        if s == 95:
            order.append((s, ("xs",)))
        if 96 <= s < 98:
            order.append((s, ("p", s - 96)))
        if s == 98:
            order.append((s, ("ps",)))
    order += [(SLOTS, ("y", m)) for m in range(KD)]
    for s, job in order:
        TJOBS.setdefault(s, []).append(job)
        TINDEX[job] = n
        n += 1


_plan_tjobs()
SJOBS = {}
SINDEX = {}


def _plan_sjobs():
    n = 0
    for s in range(SLOTS):
        jobs = []
        if s in S_AT:
            jobs.append(("piece", S_AT[s]))
        if s - 1 in KT_AT:
            jobs.append(("cache", s - 1))
        if s in (61, 62):
            jobs.append(("new", s - 61))
        for job in jobs:
            SJOBS.setdefault(s, []).append(job)
            SINDEX[job] = n
            n += 1


_plan_sjobs()


def small_steps(s):
    t, sc = TJOBS.get(s, []), SJOBS.get(s, [])
    steps = [("transposes", x) for x in t if x[0] == "qk"] + [("scores", x) for x in sc if x[0] == "piece"]
    steps += [("transposes", x) for x in t if x[0] != "qk"] + [("scores", x) for x in sc if x[0] != "piece"]
    if s - 2 in S_AT:
        steps.append(("values", S_AT[s - 2]))
    if V_SLOT0 <= s < V_SLOT0 + NBUF:
        steps.append(("sample_values", s - V_SLOT0))
    return steps


STEPS = {s: small_steps(s) for s in range(SLOTS)}


def build(nc, t):
    ctx = ExitStack()
    with ctx:
        base = (nc.sbuf_base + 31) // 32 * 32
        A_H = 0
        A_W = A_H + 2 * KD * NT * 4
        A_C = A_W + 2 * 4096 + 4 * 8192
        A_QK = A_C + 4 * NT * 4
        A_QK1 = A_QK + KD * NT * 4
        A_V = A_QK1 + KD * NT * 4
        A_O = A_V + KD * NT * 4
        OB = 4 * H * 66 * 4
        A_F = A_O + 3 * OB
        A_X = A_O + KD * NT * 4
        A_R = A_F + 4096 + 8192
        A_S = A_R + 16384 + 4096
        ends = [0]

        def sb(name, shape, dt, at):
            size = int(np.prod(shape[1:])) * (2 if dt == BF16 else 4)
            ends[0] = max(ends[0], at + size)
            return nc.alloc_sbuf_tensor_at(name, shape, dt, offset=base + at)

        h_hi = sb("h_hi", [128, KD, NT], F32R, A_H)
        h_lo = sb("h_lo", [128, KD, NT], F32R, A_H + KD * NT * 4)
        w_raw = sb("w_raw", [128, 2, 1024], F32, A_W)
        w_hi = sb("w_hi", [128, 2, 2048], F32R, A_W + 8192)
        w_lo = sb("w_lo", [128, 2, 2048], F32R, A_W + 8192 + 16384)
        z = sb("z", [128, 2, NT], F32, A_C)
        sq = sb("sq", [128, 2, NT], F32, A_C + 2 * NT * 4)
        qT = [sb(f"qT{g}", [128, 4, SEQ], F32, (A_QK, A_QK1)[g]) for g in range(2)]
        kT = [sb(f"kT{g}", [128, 4, SEQ], F32, (A_QK, A_QK1)[g] + 4 * SEQ * 4) for g in range(2)]
        x2_hi = sb("x2_hi", [128, KD, NT], F32R, A_QK)
        x2_lo = sb("x2_lo", [128, KD, NT], F32R, A_V)
        va = sb("va", [128, 4, DA], F32, A_QK1)
        uT = sb("uT", [128, 4, NT], F32, A_QK1 + 4 * DA * 4)
        mA = sb("mA", [128, KD, NT], F32, A_QK1)
        proj = sb("proj", [128, KD, NT], F32, A_QK1)
        V = [sb(f"V{g}", [128, 4, H, HD + 1], F32, A_V + 4 * NT * 4 * g) for g in range(2)]
        late = A_V + 4 * NT * 4
        gv_b = sb("gv_b", [128, DA], F32, late)
        bs_b = sb("bs_b", [128, 4, 128], F32, late + 2048)
        wsT = sb("wsT", [128, 4, 128], F32, late + 4096)
        smask = sb("smask", [128, NG * 160], F32, late + 6144)
        wsS = sb("wsS", [128, 4, NS], F32, late + 8064)[NG * NS:128]
        wsT4 = sb("wsT4", [128, 4, T], F32, late + 8576)[NG * NS:128]
        O_blk = sb("O_blk", [128, 4, H, 66], F32, A_O)
        O2 = sb("O2", [128, 4, H, 66], F32, A_O)
        O0 = sb("O0", [128, 4, H, 66], F32, A_O + OB)
        O1 = sb("O1", [128, 4, H, 66], F32, A_O + 2 * OB)
        b_nat = sb("b_nat", [128, 4, H * HD], F32, A_O + 2 * OB)
        ws_nat = sb("ws_nat", [128, 4, 128], F32, A_O)
        ws_tril = sb("ws_tril", [128, 4, 128], F32, A_O + 2048)
        thb = sb("thb", [128, KD, NT], F32, A_O)
        hf = sb("hf", [128, 2, NT], F32, A_O)
        rb = sb("rb", [128, NT], F32, A_O + 2 * NT * 4)
        ss = sb("ss", [128, NT], F32, A_O + 3 * NT * 4)
        sqf = sb("sqf", [128, 2, NT], F32, A_O + 4 * NT * 4)
        xT = sb("xT", [128, KD, NT], F32, A_X)
        fin = sb("fin", [128, 2, 512], F32, A_F)
        prob = sb("prob", [128, 2, 512], F32, A_F + 4096)
        PT = sb("PT", [128, 2, 512], F32, A_F + 8192)
        tha = sb("tha", [128, 4, NT], F32, A_F)
        cache = sb("cache", [128, 2, 4, 512], F32, A_R)
        KT = sb("KT", [128, 2, 512], F32, A_R + 16384)
        smp = [sb(f"smp{x}", [128, NG * 160], F32, A_R + 16384 + 1920 * x) for x in range(2)]
        xn = sb("xn", [128, 4, D], F32, A_R)
        xs = sb("xs", [NS, D], F32, A_R + 16384)
        pT_hi = sb("pT_hi", [128, 2, NT], F32R, A_R)
        pT_lo = sb("pT_lo", [128, 2, NT], F32R, A_R + 2 * NT * 4)
        pn = sb("pn", [128, 4, DPLE], F32, A_S)
        pns = sb("pns", [NS, DPLE], F32, A_S + 4096)
        at = A_S
        qb = sb("qb", [128, NG * 4, 2, NS], F32, at); at += NG * 4 * 2 * NS * 4
        kn = sb("kn", [128, NG * 4, NS], F32, at); at += NG * 4 * NS * 4
        vn = sb("vn", [128, 512], F32, at); at += 2048
        vas = vn[NG * NS:128]
        Sc = sb("Sc", [128, NG, 256], F32, at); at += NG * 1024
        Sn = sb("Sn", [NG * NS, 256], F32, at); at += 1024
        A_K = at
        ident = sb("ident", [128, 128], F32, A_K)
        identb = sb("identb", [128, 128], BF16, A_K + 512)
        masks = sb("masks", [128, 5, 128], BF16, A_K + 768)
        ones = sb("ones", [128, 128], F32, A_K + 2304)
        cs = sb("cs", [128, 5, 2, 16], F32, A_K + 2816)
        gq_b = sb("gq_b", [128, HD], F32, A_K + 3456)
        gk_b = sb("gk_b", [128, HD], F32, A_K + 3712)
        gcol = sb("gcol", [128, 3, KD], F32, A_K + 3968)
        mhalf = sb("mhalf", [128, 32], F32, A_K + 4064)
        st = sb("st", [128, 2, 32], F32, A_K + 4192)
        al = sb("al", [128, NG, 32], F32, A_K + 4448)
        mx = sb("mx", [128, 32], F32, A_K + 4832)
        rot = sb("rot", [128, 8, 16], F32, A_K + 4960)
        rot2 = sb("rot2", [128, 8, 16], F32, A_K + 5472)
        tril = sb("tril", [128, 128], F32, A_K + 5984)
        same_b = sb("same_b", [128, NS], F32, A_K + 6496)[NG * NS:128]
        assert base + ends[0] <= nc.sbuf_usable_end, (base + ends[0], nc.sbuf_usable_end)

        def pb(name, shape):
            return ctx.enter_context(nc.psum_tensor(name, shape, F32))

        gm = pb("gm", [128, 4, 512])
        psS = pb("psS", [128, 512])
        psT = pb("psT", [128, 2, 512])
        psO = pb("psO", [128, 512])

        def sem(name):
            return ctx.enter_context(nc.semaphore(name))

        w_landed = [sem("w_landed0"), sem("w_landed1")]
        w_hi_done, w_lo_done = sem("w_hi_done"), sem("w_lo_done")
        unit_ready, unit_out, z_used = sem("unit_ready"), sem("unit_out"), sem("z_used")
        sq_ready, ssq_ready, rstd_ready = sem("sq_ready"), sem("ssq_ready"), sem("rstd_ready")
        fin_ready = sem("fin_ready")
        fin_stored = [sem("fin_stored0"), sem("fin_stored1")]
        gelu_arg, gelu_tanh = sem("gelu_arg"), sem("gelu_tanh")
        v_stored = [sem(f"v_stored{g}") for g in range(NG)]
        t_ready, t_out, s_ready, s_used = sem("t_ready"), sem("t_out"), sem("s_ready"), sem("s_used")
        exp_done, pv_ready, o_out = sem("exp_done"), sem("pv_ready"), sem("o_out")
        o_moved = sem("o_moved")
        cache_landed = [sem("cache_landed0"), sem("cache_landed1")]
        cache_kept = [sem("cache_kept0"), sem("cache_kept1")]
        cache_used = sem("cache_used")
        cache_copied = sem("cache_copied")
        MERGED = {UNIT["ob", m]: m for m in range(KD)}
        smp_masked, smp_exp, smp_norm, smp_b = sem("smp_masked"), sem("smp_exp"), sem("smp_norm"), sem("smp_b")
        va_sq, va_rstd, va_done, va_stored = sem("va_sq"), sem("va_rstd"), sem("va_done"), sem("va_stored")
        mix_done, ab_hi, ab_lo = sem("mix_done"), sem("ab_hi"), sem("ab_lo")
        al_arg, al_exp, o1_scaled, b_ready = sem("al_arg"), sem("al_exp"), sem("o1_scaled"), sem("b_ready")
        ws_done, ws_rows = sem("ws_done"), sem("ws_rows")
        const1_in, x_tile_in = sem("const1_in"), [sem(f"x_tile_in{a}") for a in range(4)]
        const_in, const2_in, x_in, x_sq, x_rstd, x_scaled = (sem("const_in"), sem("const2_in"), sem("x_in"), sem("x_sq"),
                                                             sem("x_rstd"), sem("x_scaled"))
        x_scaled2 = sem("x_scaled2")
        tmp_out = sem("tmp_out")
        h_hi_done, h_lo_done = sem("h_hi_done"), sem("h_lo_done")
        x2_in, p_in = sem("x2_in"), sem("p_in")
        xsq, ss_done, hid_hi, hid_lo = sem("xsq"), sem("ss_done"), sem("hid_hi"), sem("hid_lo")
        n_sum, n_ms, n_pow, n_diag, gate_tanh = (sem("n_sum"), sem("n_ms"), sem("n_pow"), sem("n_diag"), sem("gate_tanh"))
        zeroed, y_nat, y_stored = sem("zeroed"), sem("y_nat"), sem("y_stored")
        dve_step, pool_step, act_step = sem("dve_step"), sem("pool_step"), sem("act_step")

        def wview(p, hh, j=None):
            if j is not None:
                if p < 4:
                    w, r0, c0 = t["w_ff1"], 0, j * 1024 + p * 256
                    v = w.rearrange("(k p) n -> p k n", p=128)
                else:
                    v = t["w_ff2"].rearrange("(k p) n -> p k n", p=128)
                    r0, c0 = j * 8, (p - 4) * 256
                return v[:, bass.ds(r0 + 4 * hh, 4), bass.ds(c0, 256)]
            if p >= P_PG:
                kind, g, i = "pg", 0, p - P_PG
            else:
                kind, g, i = PANELS[p]
            name, c0 = {"k": ("w_in", 2 * DA + QKV + g * 512 + i * 256), "q": ("w_in", 2 * DA + g * 512 + i * 256),
                        "v": ("w_in", 2 * DA + 2 * QKV + g * 512 + i * 256), "va": ("w_in", DA + i * 256), "u": ("w_in", i * 256),
                        "ga": ("w_in", 2 * DA + 3 * QKV + i * 256), "gb": ("w_in", 2 * DA + 3 * QKV + D + i * 256),
                        "oa": ("w_oa", i * 512), "ob": ("w_ob", i * 512), "wo": ("w_o", i * 256),
                        "pj": ("w_ple_proj", 0), "pg": ("w_ple_gate", i * 256)}[kind]
            n = COLS.get(kind, 256)
            nk = 1024 // n
            return t[name].rearrange("(k p) n -> p k n", p=128)[:, hh * nk:(hh + 1) * nk, c0:c0 + n]

        def residue(ap2, a):
            return ap2.rearrange("p (i a) -> p a i", a=4)[:, a]

        def tokens(ap3, k, tile, residues):
            if residues:
                return residue(ap3[:, k, 0:SEQ], tile)
            return ap3[:, k, tile * 128:(tile + 1) * 128]

        CONSTS1, CONSTS, CONSTS2 = 16 * 4, 16 * 6, 16 * 5

        def bc(ap, axis, n):
            v = ap.unsqueeze(axis)
            shape = list(v.shape)
            shape[axis] = n
            return v.broadcast_to(shape)

        def cache_loads(n, kv):
            g, b = BUFS[n]
            src = t[f"cache{g}"][:, kv]
            dst = cache[:, n % 2]
            if g == 0:
                return [(dst, src[b:b + 4].rearrange("b p f -> p b f"))]
            if g == 1:
                return [(dst, src[b].rearrange("(i r) f -> i r f", r=4))]
            out = []
            for bb in range(2):
                v = src[b + bb].rearrange("(i r) f -> i r f", r=16)
                for e in range(2):
                    out.append((cache[64 * e:64 * e + 64, n % 2, 2 * bb:2 * bb + 2], v[:, e:4:2]))
            return out

        def cache_stores(n, kv):
            g, b = BUFS[n]
            if g == 2:
                return []
            dst = t[f"kvs{g}"][:, kv]
            out = []
            if g == 0:
                for lo, hi in ((16, 128), (4, 16)):
                    out.append((dst[b:b + 4, lo - T:hi - T].rearrange("b p f -> p b f"), cache[lo:hi, n % 2]))
            else:
                v = dst[b].rearrange("(i r) f -> i r f", r=4)
                for lo, hi in ((16, 128), (1, 16)):
                    out.append((v[lo - 1:hi - 1], cache[lo:hi, n % 2]))
            return out

        def landed_count(q):
            return sum(16 * (4 if BUFS[x % NBUF][0] == 2 else 1) for x in range(q % 2, q + 1, 2))

        def kept_count(q):
            return sum(16 * (0 if BUFS[x % NBUF][0] == 2 else 2) for x in range(q % 2, q + 1, 2))

        K_LAST = {}
        for s_, job in KT_AT.items():
            K_LAST[job[4]] = max(s_, K_LAST.get(job[4], 0))

        V_STORES = [16 * 4, 16 * 10, 16 * 10]
        FIN_STORES = [0, 0]
        for u in range(U_FF):
            if stores_keys(u):
                FIN_STORES[kqn(u) % 2] += 16

        def fin_count(n):
            return sum(16 for u in range(U_FF) if stores_keys(u) and kqn(u) <= n and kqn(u) % 2 == n % 2)

        block = ctx.enter_context(nc.Block())

        @block.sync
        def _(sp):
            def load_panel(p, j=None, pp=None):
                pp = p if pp is None else pp
                for hh in range(2):
                    if not (isinstance(pp, int) and pp == 0):
                        sp.wait_ge(w_lo_done, 2 * (pp - 1) + hh + 1)
                    nk = 1024 // (256 if j is not None or p >= P_PG else COLS.get(PANELS[p][0], 256))
                    sp.dma_start(w_raw[:, hh].rearrange("p (k n) -> p k n", k=nk), wview(p, hh, j)).then_inc(w_landed[hh], 16)

            def load_cache(q):
                if q >= NBUF + 2:
                    sp.wait_ge(cache_used, q - NBUF - 1)
                elif q >= 2:
                    last = K_LAST[q - 2]
                    sp.wait_ge(t_ready, TINDEX[("kt", last, KT_AT[last][3] - 1)] + 1)
                if q >= 2:
                    if kept_count(q - 2):
                        sp.wait_ge(cache_kept[q % 2], kept_count(q - 2))
                for dst, src in cache_loads(q % NBUF, q // NBUF):
                    sp.dma_start(dst, src).then_inc(cache_landed[q % 2], 16)

            def keep_cache(q):
                ops = cache_stores(q % NBUF, q // NBUF)
                if ops:
                    sp.wait_ge(cache_landed[q % 2], landed_count(q))
                for dst, src in ops:
                    sp.dma_start(dst, src).then_inc(cache_kept[q % 2], 16)

            for a in range(4):
                sp.dma_start(xn[:, a], t["x_prompt"][128 * a:128 * a + 128]).then_inc(x_tile_in[a], 16)
            sp.dma_start(xs[:], t["x_sample"]).then_inc(x_in, 16)
            sp.dma_start(ident[:], t["c_ident"]).then_inc(const1_in, 16)
            for i, name in enumerate(("g_mix", "g_ffn", "g_ple")):
                sp.dma_start(gcol[:, i], t[name].rearrange("(k p) -> p k", p=128),
                             allow_slow_non_contiguous=True).then_inc(const1_in, 16)
            load_panel(0)
            for dst, name in ((identb, "c_identb"), (cs, "c_rot"), (masks, "c_masks"), (tril, "c_tril")):
                sp.dma_start(dst[:], t[name]).then_inc(const_in, 16)
            for dst, name in ((gq_b, "g_q"), (gk_b, "g_k")):
                sp.dma_start(dst[:], t[name].partition_broadcast(128)).then_inc(const_in, 16)
            for s in range(SLOTS):
                p, kind, g, i, sub = UNITS[s]
                if sub == 0 and p + 1 < len(PANELS):
                    load_panel(p + 1)
                if s == 10:
                    sp.wait_ge(t_out, KD + 1)
                    load_cache(0)
                    load_cache(1)
                for q in range(NBUF):
                    if K_LAST[q] + 1 == s:
                        keep_cache(q)
                        if q + 2 < NBUF:
                            load_cache(q + 2)
                        else:
                            load_cache(q + 2)
                q = s - V_SLOT0 + NBUF
                if NBUF <= q - 1 < 2 * NBUF:
                    keep_cache(q - 1)
                    if q + 1 < 2 * NBUF:
                        load_cache(q + 1)
                if s == 47:
                    sp.wait_ge(pv_ready, 24)
                    sp.wait_ge(o_moved, 256)
                    sp.wait_ge(v_stored[1], V_STORES[1])
                    sp.dma_start(gv_b[:], t["g_v"].partition_broadcast(128)).then_inc(const2_in, 16)
                    sp.dma_start(bs_b[:], t["b_s"].partition_broadcast(128)).then_inc(const2_in, 16)
                    sp.dma_start(smask[:], t["c_smask"]).then_inc(const2_in, 16)
                    sp.dma_start(ws_nat[:], t["w_s"].rearrange("g t s -> t g s")).then_inc(const2_in, 16)
                    sp.dma_start(same_b, t["c_same"]).then_inc(const2_in, 16)
                if s == 54:
                    sp.wait_ge(t_out, TINDEX[("ws",)] + 1)
                    for b in range(NB):
                        sp.dma_start(wsT4[T * b:T * b + T], wsT[0:T, :, 0:T]).then_inc(ws_rows, 16)
                if s == 86:
                    sp.wait_ge(smp_b, 1)
                    sp.wait_ge(cache_kept[0], kept_count(2 * NBUF - 2))
                    sp.wait_ge(cache_kept[1], kept_count(2 * NBUF - 1))
                    sp.dma_start(xn[:], t["x_prompt"].rearrange("(b p) d -> p b d", p=128)).then_inc(x2_in, 16)
                    sp.dma_start(xs[:], t["x_sample"]).then_inc(x2_in, 16)
                    sp.wait_ge(t_out, TINDEX[("bt", 3)] + 1)
                    sp.dma_start(pn[:], t["p_prompt"].rearrange("(b p) d -> p b d", p=128)).then_inc(p_in, 16)
                    sp.dma_start(pns[:], t["p_sample"]).then_inc(p_in, 16)
            def hidden_group(j, final=False):
                for q in range(FF_PANELS):
                    load_panel(q, j, j * FF_PANELS + (P_FF + q))

            with sp.Fori(0, NFF - 1) as j:
                hidden_group(j)
            hidden_group(NFF - 1, final=True)
            for i in range(4):
                load_panel(P_PG + i, None, P_PG + i)
            sp.wait_ge(cache_copied, 16 * 64)
            sp.wait_ge(fin_stored[0], FIN_STORES[0])
            sp.wait_ge(fin_stored[1], FIN_STORES[1])
            for g in range(NG):
                sp.wait_ge(v_stored[g], V_STORES[g])
            sp.wait_ge(va_stored, 16 * 2)
            sp.wait_ge(y_stored, 16 * 4)

        @block.scalar
        def _(act):
            steps = [0]

            def link(ins):
                steps[0] += 1
                ins.then_inc(act_step, 1)
                act.wait_ge(act_step, steps[0])

            def split_hi(pp, r, free):
                for hh in range(2):
                    act.wait_ge(w_landed[hh], (pp + 1) * 16)
                    if hh == 0 and free is not None:
                        act.wait_ge(unit_ready, free)
                    nc.scalar.copy(w_hi[:, r, hh * 1024:(hh + 1) * 1024], w_raw[:, hh]).then_inc(w_hi_done, 1)

            def stage_slot(u):
                n = zc(u)
                if n > 2:
                    act.wait_ge(z_used, n - 2)
                    prev = [x for x in range(u) if zc(x) == n - 2 and STAGED[x]][0]
                    if UNITS[prev][1] in ("k", "q"):
                        act.wait_ge(fin_ready, kqn(prev) + 1)
                return (n - 1) % 2

            def evacuate(u):
                p, kind, g, i, sub = UNITS[u]
                act.wait_ge(unit_ready, u + 1)
                if kind in NATURAL:
                    rows = 128 if sub < 2 else NS
                    n = 512 if sub < 2 else 256
                    src = gm[0:rows, u % 4, 0:n]
                else:
                    src = gm[:, 2 * (u % 2):2 * (u % 2) + 2, 0:HALF]

                def two(ap):
                    return ap.rearrange("p (n c) -> p n c", n=2)

                if u == 0:
                    act.wait_ge(h_lo_done, KD + 1)
                if kind in ("k", "q", "va"):
                    r = stage_slot(u)
                    nc.scalar.activation(sq[0:rows, r, 0:n], src, ACT.Square).then_inc(sq_ready, 1)
                    nc.scalar.copy(z[0:rows, r, 0:n], src).then_inc(unit_out, 1)
                elif kind == "u":
                    r = stage_slot(u)
                    nc.scalar.activation(two(sq[:, r]), src, ACT.Square).then_inc(sq_ready, 1)
                    nc.scalar.copy(two(z[:, r]), src).then_inc(unit_out, 1)
                elif kind == "v":
                    if sub < 2:
                        if g == 2 and i == 0 and sub == 0:
                            act.wait_ge(v_stored[0], V_STORES[0])
                            act.wait_ge(pv_ready, 16)
                        nc.scalar.copy(V[g % 2][:, 2 * sub:2 * sub + 2, 4 * i:4 * i + 4, 0:HD],
                                       src.rearrange("p (t h d) -> p t h d", t=2, h=4)).then_inc(unit_out, 1)
                    else:
                        nc.scalar.copy(vn[NS * g:NS * g + NS, 256 * i:256 * i + 256], src).then_inc(unit_out, 1)
                    act.wait_ge(unit_out, u + 1)
                    cols = slice(256 * i, 256 * i + 256)
                    if sub == 2:
                        dst = t[f"kvs{g}"][:, 1, WIN[g] - T:WIN[g], cols]
                        act.dma_start(dst, vn[NS * g:NS * g + NS, cols]).then_inc(v_stored[g], 16)
                    elif g > 0:
                        dst = t[f"kvp{g}"][1, :, cols].rearrange("(i a) (h d) -> i a h d", a=4, h=4)[:, 2 * sub:2 * sub + 2]
                        for x in range(2):
                            act.dma_start(dst[:, x], V[g % 2][:, 2 * sub + x, 4 * i:4 * i + 4, 0:HD]).then_inc(v_stored[g], 16)
                    elif sub == 1:
                        dst = t["kvp0"][1, :, cols].rearrange("i (h d) -> i h d", h=4)
                        act.dma_start(dst, V[0][:, 3, 4 * i:4 * i + 4, 0:HD]).then_inc(v_stored[g], 16)
                elif kind in ("ga", "gb"):
                    if kind == "ga":
                        m = 2 * i + sub
                        if m == 0:
                            act.wait_ge(exp_done, 32)
                            act.wait_ge(pv_ready, 32)
                            act.wait_ge(va_sq, 5)
                        if m == 4:
                            act.wait_ge(z_used, zc(UNIT["oa", 3]))
                        out = tha[:, m % 4]
                    else:
                        m = 2 * i + sub
                        if m == 0:
                            act.wait_ge(b_ready, 1)
                            act.wait_ge(t_ready, TINDEX[("bt", 3)] + 1)
                        out = thb[:, m]
                    nc.scalar.activation(two(out), src, ACT.Tanh, scale=0.5).then_inc(unit_out, 1)
                elif kind == "pj":
                    if sub == 0:
                        act.wait_ge(h_lo_done, HP)
                    nc.scalar.copy(two(proj[:, sub]), src).then_inc(unit_out, 1)
                else:
                    r = stage_slot(u)
                    nc.scalar.copy(two(z[:, r]), src).then_inc(unit_out, 1)
                if kind == "wo":
                    m = 2 * i + sub
                    if m == 0:
                        act.wait_ge(ab_lo, 9)
                    square_x(m, m, zc(u))

            def merged_hi(m):
                act.wait_ge(z_used, zc(UNIT["ob", m]))
                nc.scalar.mul(h_hi[:, m], mA[:, m], 0.5).then_inc(h_hi_done, 1)

            def square_x(m, n, zu):
                act.wait_ge(z_used, zu)
                if n >= 2:
                    act.wait_ge(ss_done, n - 1)
                nc.scalar.activation(sq[:, m % 2], xT[:, m], ACT.Square).then_inc(xsq, 1)

            def gained_hi(n, m, zu):
                act.wait_ge(z_used, zu)
                nc.scalar.activation(h_hi[:, m], xT[:, m], ACT.Copy, scale=gcol[:, n + 1, m:m + 1]).then_inc(h_hi_done, 1)

            def take_transposes(job):
                n = TINDEX[job]
                act.wait_ge(t_ready, n + 1)
                src = psT[:, n % 2]
                kind = job[0]
                if kind == "h":
                    k = job[1]
                    act.wait_ge(const1_in, CONSTS1)
                    nc.scalar.activation(h_hi[:, k, 0:SEQ], src, ACT.Copy, scale=gcol[:, 0, k:k + 1]).then_inc(h_hi_done, 1)
                    if k == 3:
                        split_hi(0, 0, None)
                elif kind == "hs":
                    act.wait_ge(t_out, n + 1)
                    nc.scalar.copy(h_hi[:, :, SEQ:NT], sq[:, 0, 0:KD * NS].rearrange("p (k n) -> p k n", k=KD)).then_inc(h_hi_done, KD)
                elif kind == "qk":
                    u = job[1]
                    _, qk, g, i, sub = UNITS[u]
                    if sub < 2:
                        dst = (qT if qk == "q" else kT)[g % 2][:, 2 * i:2 * i + 2, 256 * sub:256 * sub + 256]
                        if g == 2 and i == 0 and sub == 0:
                            act.wait_ge(s_ready, SINDEX[("piece", 15)] + 1)
                        nc.scalar.copy(dst, src.rearrange("p (c n) -> p c n", c=2)).then_inc(t_out, 1)
                    elif qk == "k":
                        nc.scalar.copy(kn[:, 4 * g + 2 * i:4 * g + 2 * i + 2],
                                       src[:, 0:2 * NS].rearrange("p (c n) -> p c n", c=2)).then_inc(t_out, 1)
                    else:
                        act.wait_ge(zeroed, 1)
                        v = src[:, 0:2 * NS].rearrange("p (c n) -> p c n", c=2)
                        link(nc.scalar.copy(qb[0:64, 4 * g + 2 * i:4 * g + 2 * i + 2, 0], v[0:64]))
                        nc.scalar.copy(qb[64:128, 4 * g + 2 * i:4 * g + 2 * i + 2, 1], v[64:128]).then_inc(t_out, 1)
                    if qk == "k":
                        act.wait_ge(fin_ready, kqn(u) + 1)
                        f = fin[:, kqn(u) % 2]
                        cols = slice(256 * i, 256 * i + 256)
                        done = fin_stored[kqn(u) % 2]
                        if sub == 2:
                            act.dma_start(t[f"kvs{g}"][:, 0, WIN[g] - T:WIN[g], cols], f[0:NS, 0:256]).then_inc(done, 16)
                        elif g == 0:
                            if sub == 1:
                                act.dma_start(t["kvp0"][0, :, cols], f[:, 256:512]).then_inc(done, 16)
                        else:
                            dst = t[f"kvp{g}"][0, :, cols].rearrange("(b p) f -> p b f", p=128)[:, 2 * sub:2 * sub + 2]
                            act.dma_start(dst, f.rearrange("p (a f) -> p a f", a=2)).then_inc(done, 16)
                elif kind == "pt":
                    j = job[1]
                    c0 = 128 if PIECES[j][0] == 0 and PIECES[j][2] == 0 else 0
                    if j >= 2:
                        act.wait_ge(pv_ready, j - 1)
                    nc.scalar.copy(PT[:, j % 2, c0:512], src[:, c0:512]).then_inc(t_out, 1)
                elif kind == "kt":
                    s, x = job[1], job[2]
                    prev = [y for y in KT_AT if y < s]
                    if prev:
                        act.wait_ge(s_ready, SINDEX[("cache", max(prev))] + 1)
                    nc.scalar.copy(KT[:, x], src).then_inc(t_out, 1)
                elif kind == "ws":
                    nc.scalar.copy(wsT[:], src.rearrange("p (g n) -> p g n", g=4)).then_inc(t_out, 1)
                elif kind == "ss":
                    nc.scalar.copy(smp[job[1]][:], src[:, 0:480]).then_inc(t_out, 1)
                elif kind in ("pa", "pb"):
                    hf_ = job[1]
                    v = src[:, 0:384].rearrange("p (g n) -> p g n", g=3)
                    if kind == "pa":
                        nc.scalar.copy(Sc[:, :, 128 * hf_:128 * hf_ + 128], v).then_inc(t_out, 1)
                    else:
                        nc.scalar.copy(Sn[:, 128 * hf_:128 * hf_ + 128], src[0:NG * NS, 0:128]).then_inc(t_out, 1)
                elif kind == "mix":
                    g = job[1]
                    act.wait_ge(z_used, zc(UNIT["u", 3]))
                    if g >= 2:
                        act.wait_ge(mix_done, g - 1)
                    nc.scalar.copy(sq[:, g % 2, 0:SEQ], src).then_inc(t_out, 1)
                elif kind == "mixs":
                    act.wait_ge(mix_done, 3)
                    nc.scalar.copy(sq[:, 0, 0:4 * NS], src[:, 0:4 * NS]).then_inc(t_out, 1)
                elif kind == "bt":
                    c = job[1]
                    act.wait_ge(ab_lo, 4 + c - 1 if c >= 2 else 4)
                    nc.scalar.copy(x2_hi[:, 4 + c, 0:SEQ].rearrange("p (i a) -> p a i", a=4),
                                   src.rearrange("p (a i) -> p a i", a=4)).then_inc(ab_hi, 1)
                    nc.scalar.copy(sq[:, c % 2, 0:SEQ], src).then_inc(t_out, 1)
                elif kind == "x":
                    k = job[1]
                    nc.scalar.copy(xT[:, k, 0:SEQ], src).then_inc(t_out, 1)
                elif kind == "xs":
                    nc.scalar.copy(xT[:, :, SEQ:NT], src[:, 0:KD * NS].rearrange("p (k n) -> p k n", k=KD)).then_inc(t_out, 1)
                elif kind == "p":
                    k = job[1]
                    act.wait_ge(z_used, zc(UNIT["ob", 7]))
                    nc.scalar.copy(pT_hi[:, k, 0:SEQ], src).then_inc(h_hi_done, 1)
                    nc.scalar.copy(sqf[:, k, 0:SEQ], src).then_inc(t_out, 1)
                elif kind == "ps":
                    act.wait_ge(h_lo_done, HP + 2)
                    v = src[:, 0:2 * NS].rearrange("p (k n) -> p k n", k=2)
                    nc.scalar.copy(pT_hi[:, :, SEQ:NT], v).then_inc(h_hi_done, 1)
                    nc.scalar.copy(sqf[:, 0, 0:2 * NS].rearrange("p (k n) -> p k n", k=2), v).then_inc(t_out, 1)

            for a in range(4):
                act.wait_ge(x_tile_in[a], 16)
                nc.scalar.activation(gm[:, 0:2].rearrange("p b n -> p (b n)"), xn[:, a], ACT.Square,
                                     accum_out=st[:, 0, a:a + 1]).then_inc(x_sq, 1)
                act.wait_ge(x_sq, a + 1)
            act.wait_ge(x_in, 16)
            nc.scalar.activation(gm[0:NS, 0:2].rearrange("p b n -> p (b n)"), xs[:], ACT.Square,
                                 accum_out=st[0:NS, 0, 4:5]).then_inc(x_sq, 1)
            act.wait_ge(x_rstd, 1)
            nc.scalar.activation(xn[:, 3], xn[:, 3], ACT.Copy, scale=st[:, 0, 3:4]).then_inc(x_scaled2, 1)
            nc.scalar.activation(xs[:], xs[:], ACT.Copy, scale=st[0:NS, 0, 4:5]).then_inc(x_scaled2, 1)
            for job in TJOBS[-1]:
                take_transposes(job)
            for s in range(SLOTS):
                p, kind, g, i, sub = UNITS[s]
                if sub == 0:
                    split_hi(p + 1, (p + 1) % 2, panel_end(p - 1) if p >= 1 else None)
                if s - 1 in MERGED:
                    merged_hi(MERGED[s - 1])
                evacuate(s)
                if kind == "pj":
                    if sub == 0:
                        act.wait_ge(unit_ready, UNIT["wo", 7] + 1)
                    gained_hi(0, sub, zc(UNIT["wo", sub]))
                if kind in ("va", "u"):
                    act.wait_ge(gelu_arg, GELU.index(s) + 1)
                    r = (zc(s) - 1) % 2
                    rows, n = (128, NT) if kind == "u" else (128, 512) if sub < 2 else (NS, 256)
                    nc.scalar.activation(sq[0:rows, r, 0:n], sq[0:rows, r, 0:n], ACT.Tanh, scale=GELU_B).then_inc(gelu_tanh, 1)
                for job in TJOBS.get(s, []):
                    take_transposes(job)
                if s in S_AT:
                    j = S_AT[s]
                    act.wait_ge(s_used, SINDEX[("piece", j)] + 1)
                    nc.scalar.activation(prob[:, j % 2], prob[:, j % 2], ACT.Exp, scale=SCALE).then_inc(exp_done, 1)
                if s == 62:
                    act.wait_ge(t_ready, TINDEX[("qk", 47)] + 1)
                    act.wait_ge(fin_stored[0], FIN_STORES[0])
                    act.wait_ge(fin_stored[1], FIN_STORES[1])
                    act.wait_ge(z_used, zc(59))
                    for a in range(5):
                        src = va[:, a] if a < 4 else vas
                        rows = slice(0, 128) if a < 4 else slice(NG * NS, 128)
                        nc.scalar.activation(fin[rows, 0], src, ACT.Square, accum_out=st[rows, 1, a:a + 1]).then_inc(va_sq, 1)
                        act.wait_ge(va_sq, a + 1)
                if s == 64:
                    act.wait_ge(va_done, 5)
                    act.dma_start(t["cvp"], va[:, 3]).then_inc(va_stored, 16)
                    act.dma_start(t["cvs"], vas).then_inc(va_stored, 16)
                if s == 64:
                    act.wait_ge(al_arg, 1)
                    nc.scalar.activation(al[:], al[:], ACT.Exp, scale=SCALE).then_inc(al_exp, 1)
                    for hf_ in range(2):
                        act.wait_ge(smp_masked, hf_ + 1)
                        nc.scalar.activation(smp[hf_][:], smp[hf_][:], ACT.Exp, scale=SCALE,
                                             accum_out=st[:, 0, 8 + hf_:9 + hf_]).then_inc(smp_exp, 1)
                if s == 65:
                    act.wait_ge(mix_done, 5)
                    act.wait_ge(s_ready, SINDEX[("piece", 31)] + 1)
                    for g_ in range(4):
                        nc.scalar.copy(x2_hi[:, g_], uT[:, g_]).then_inc(ab_hi, 1)
                if s == V_SLOT0 + NBUF:
                    act.wait_ge(smp_b, 1)
                    nc.scalar.copy(x2_hi[:, 4:8, SEQ:NT], sq[:, 0, 0:4 * NS].rearrange("p (c n) -> p c n", c=4)).then_inc(ab_hi, 1)
            def take_y(m):
                n = TINDEX[("y", m)]
                act.wait_ge(t_ready, n + 1)
                nc.scalar.copy(xs[:, 128 * m:128 * m + 128], psO[0:NS, 0:128]).then_inc(y_nat, 1)
                nc.scalar.copy(xn[:, :, 128 * m:128 * m + 128], psT[:, n % 2].rearrange("p (a n) -> p a n", a=4)).then_inc(t_out, 1)
                if m % 4 == 3:
                    cols = slice(128 * (m - 3), 128 * (m + 1))
                    act.wait_ge(y_nat, m + 1)
                    act.wait_ge(t_out, n + 1)
                    act.dma_start(t["y_prompt"].rearrange("(b p) d -> p b d", p=128)[:, :, cols], xn[:, :, cols]).then_inc(y_stored, 16)
                    act.dma_start(t["y_sample"][:, cols], xs[:, cols]).then_inc(y_stored, 16)

            def hidden_group(j, final=False):
                for q in range(FF_PANELS):
                    pp = j * FF_PANELS + (P_FF + q)
                    split_hi(pp + 1, (P_FF + q + 1) % 2, j * FF_UNITS + (U_FF + 2 * q))
                    for sub in range(2):
                        uu = q * 2 + sub
                        u = j * FF_UNITS + (U_FF + uu)
                        zu = j * FF_UNITS + (zc(U_FF) + uu)
                        if q < 4:
                            m = uu
                            act.wait_ge(unit_ready, u + 1)
                            if uu == 0:
                                act.wait_ge(unit_out, u)
                            src = gm[:, 2 * (uu % 2):2 * (uu % 2) + 2, 0:HALF]
                            r = (zc(U_FF) - 1 + uu) % 2
                            act.wait_ge(z_used, zu - 2)
                            nc.scalar.activation(z[:, r].rearrange("p (n c) -> p n c", n=2), src, ACT.Relu).then_inc(unit_out, 1)
                            act.wait_ge(unit_out, u + 1)
                            nc.scalar.activation(x2_hi[:, m], z[:, r], ACT.Square).then_inc(hid_hi, 1)
                        elif final:
                            m = uu - 8
                            square_x(m, KD + m, zu)
                            gained_hi(1, m, zu)

            with act.Fori(0, NFF - 1) as j:
                hidden_group(j)
            hidden_group(NFF - 1, final=True)
            for i in range(4):
                if i < 3:
                    split_hi(P_PG + i + 1, (P_PG + i + 1) % 2, U_PG + 2 * i)
                for sub in range(2):
                    u = U_PG + 2 * i + sub
                    m = 2 * i + sub
                    act.wait_ge(unit_out, u + 1)
                    r = (zc(u) - 1) % 2
                    nc.scalar.activation(z[:, r], z[:, r], ACT.Tanh, scale=0.5).then_inc(gate_tanh, 1)
                    if m >= 2:
                        take_y(m - 2)
            take_y(KD - 2)
            take_y(KD - 1)

        @block.tensor
        def _(pe):
            def small_step(s, n):
                kind, what = STEPS[s][n]
                if kind == "transposes":
                    transposes(what)
                elif kind == "scores":
                    scores(what)
                elif kind == "values":
                    values(what)
                else:
                    sample_values(what)

            def between(u, g, groups):
                if u == U_PG and g == 4:
                    norm_sum(1)
                if u == U_PG + 1 and g == 2:
                    norm_spread(1)
                if 0 < u < SLOTS and u != UNIT["wo", 0]:
                    n_steps = len(STEPS[u - 1])
                    for n in range(n_steps):
                        if max(1, (n + 1) * groups // (n_steps + 1)) == g + 1:
                            small_step(u - 1, n)

            def natural_unit(u):
                p, kind, g, i, sub = UNITS[u]
                r, n = p % 2, 256
                if u >= 4:
                    pe.wait_ge(unit_out, u - 3)
                residues = kind == "v" and g > 0
                for x in range(2 if sub < 2 else 1):
                    for k in range(KD):
                        if sub < 2:
                            lh, ll = tokens(h_hi, k, 2 * sub + x, residues), tokens(h_lo, k, 2 * sub + x, residues)
                            out = gm[:, u % 4, n * x:n * x + n]
                        else:
                            if u == 2:
                                pe.wait_ge(h_lo_done, KD + 1)
                            lh, ll = h_hi[:, k, SEQ:NT], h_lo[:, k, SEQ:NT]
                            out = gm[0:NS, u % 4, 0:n]
                        wh, wl = w_hi[:, r, k * n:k * n + n], w_lo[:, r, k * n:k * n + n]
                        nc.tensor.matmul(out, lh, wh, start=k == 0, stop=False)
                        nc.tensor.matmul(out, ll, wh, start=False, stop=False)
                        last = nc.tensor.matmul(out, lh, wl, start=False, stop=k == KD - 1)
                        if x * KD + k < (2 if sub < 2 else 1) * KD - 1:
                            between(u, x * KD + k, (2 if sub < 2 else 1) * KD)
                last.then_inc(unit_ready, 1)
                return last

            def block_unit(r, n, c0, nk, b2, rh, rl, k0=0, wait_k=None, u=0):
                for k in range(nk):
                    if wait_k is not None:
                        pe.wait_ge(*wait_k(k))
                    wh = w_hi[:, r, k * n + c0:k * n + c0 + 128]
                    wl = w_lo[:, r, k * n + c0:k * n + c0 + 128]
                    for w, x, first, end in ((wh, rh, k == 0, False), (wh, rl, False, False), (wl, rh, False, k == nk - 1)):
                        for half in range(2):
                            last = nc.tensor.matmul(gm[:, 2 * b2 + half, 0:HALF], w, x[:, k0 + k, half * HALF:(half + 1) * HALF],
                                                    start=first, stop=end)
                    if k < nk - 1:
                        between(u, k, nk)
                last.then_inc(unit_ready, 1)
                return last

            def unit(u):
                p, kind, g, i, sub = UNITS[u]
                if sub == 0:
                    pe.wait_ge(w_hi_done, 2 * (p + 1))
                    pe.wait_ge(w_lo_done, 2 * (p + 1))
                if kind in NATURAL:
                    last = natural_unit(u)
                else:
                    b2 = u % 2
                    pe.wait_ge(unit_out, u if UNITS[u - 1][1] in NATURAL else u - 1)
                    n = COLS.get(kind, 256)
                    r = p % 2
                    if kind in ("u", "ga", "gb"):
                        last = block_unit(r, n, 128 * sub, KD, b2, h_hi, h_lo, u=u)
                    elif kind in ("oa", "ob"):
                        k0 = 0 if kind == "oa" else 4
                        pe.wait_ge(ab_lo, 4 if kind == "oa" else 9)
                        last = block_unit(r, n, 128 * sub, 4, b2, x2_hi, x2_lo, k0, u=u)
                    elif kind == "wo":
                        wk = (lambda k: (h_lo_done, KD + 1 + k + 1)) if (i, sub) == (0, 0) else None
                        last = block_unit(r, n, 128 * sub, KD, b2, h_hi, h_lo, 0, wk, u)
                    elif kind == "pj":
                        pe.wait_ge(h_lo_done, HP + 3)
                        last = block_unit(r, n, 128 * sub, 2, b2, pT_hi, pT_lo)

            def t_bank(job):
                n = TINDEX[job]
                if 2 <= n <= KD:
                    pe.wait_ge(h_lo_done, n - 1)
                elif n > KD:
                    pe.wait_ge(t_out, n - 1)
                return psT[:, n % 2]

            def transposes(job):
                kind = job[0]
                out = t_bank(job)
                tr = nc.tensor.transpose
                if kind in ("h", "x"):
                    k = job[1]
                    if k == 0 and kind == "h":
                        pe.wait_ge(const1_in, CONSTS1)
                        pe.wait_ge(x_scaled, 3)
                        pe.wait_ge(x_scaled2, 1)
                    elif k == 0:
                        pe.wait_ge(x2_in, 32)
                    for a in range(4):
                        last = tr(out[:, 128 * a:128 * a + 128], xn[:, a, 128 * k:128 * k + 128], ident[:])
                elif kind in ("hs", "xs"):
                    if kind == "hs":
                        pe.wait_ge(x_scaled2, 2)
                    for k in range(KD):
                        last = tr(out[:, NS * k:NS * k + NS], xs[:, 128 * k:128 * k + 128], ident[0:NS, 0:NS])
                elif kind == "p":
                    pe.wait_ge(p_in, 32)
                    k = job[1]
                    for a in range(4):
                        last = tr(out[:, 128 * a:128 * a + 128], pn[:, a, 128 * k:128 * k + 128], ident[:])
                elif kind == "ps":
                    for k in range(2):
                        last = tr(out[:, NS * k:NS * k + NS], pns[:, 128 * k:128 * k + 128], ident[0:NS, 0:NS])
                elif kind == "qk":
                    u = job[1]
                    sub = UNITS[u][4]
                    pe.wait_ge(fin_ready, kqn(u) + 1)
                    f = fin[:, kqn(u) % 2]
                    for c in range(2):
                        if sub < 2:
                            for x in range(2):
                                last = tr(out[:, 256 * c + 128 * x:256 * c + 128 * x + 128],
                                          f[:, 256 * x + 128 * c:256 * x + 128 * c + 128], ident[:])
                        else:
                            last = tr(out[:, NS * c:NS * c + NS], f[0:NS, 128 * c:128 * c + 128], ident[0:NS, 0:NS])
                elif kind == "pt":
                    j = job[1]
                    pe.wait_ge(exp_done, j + 1)
                    for b in range(4):
                        if b == 0 and PIECES[j][0] == 0 and PIECES[j][2] == 0:
                            continue
                        last = tr(out[:, 128 * b:128 * b + 128], prob[:, j % 2, 128 * b:128 * b + 128], ident[:])
                elif kind == "kt":
                    s, x = job[1], job[2]
                    g, b, r, nt, buf, t0 = KT_AT[s]
                    pe.wait_ge(cache_landed[buf % 2], landed_count(buf))
                    for c in range(4):
                        last = tr(out[:, 128 * c:128 * c + 128], cache[:, buf % 2, t0 + x, 128 * c:128 * c + 128], ident[:])
                elif kind == "ws":
                    pe.wait_ge(ws_done, 1)
                    for g in range(4):
                        last = tr(out[:, 128 * g:128 * g + 128], ws_tril[:, g], ident[:])
                elif kind == "ss":
                    hf_ = job[1]
                    pe.wait_ge(s_used, SINDEX[("new", 1)] + 1)
                    for g in range(NG):
                        tr(out[:, 128 * g:128 * g + 128], Sc[:, g, 128 * hf_:128 * hf_ + 128], ident[:])
                    last = tr(out[:, NG * 128:NG * 160], Sn[:, 128 * hf_:128 * hf_ + 128], ident[0:NG * NS, 0:NG * NS])
                elif kind == "pa":
                    hf_ = job[1]
                    pe.wait_ge(smp_norm, hf_ + 1)
                    for g in range(NG):
                        last = tr(out[:, 128 * g:128 * g + 128], smp[hf_][:, 128 * g:128 * g + 128], ident[:])
                elif kind == "pb":
                    hf_ = job[1]
                    last = tr(out[0:NG * NS, 0:128], smp[hf_][:, NG * 128:NG * 160], ident[:])
                elif kind == "mix":
                    g = job[1]
                    pe.wait_ge(va_done, 5)
                    pe.wait_ge(t_out, TINDEX[("ws",)] + 1)
                    for c in range(4):
                        last = nc.tensor.matmul(out[:, 128 * c:128 * c + 128], va[:, c, 128 * g:128 * g + 128], wsT[:, g], start=True, stop=True)
                elif kind == "mixs":
                    pe.wait_ge(ws_done, 2)
                    for g in range(4):
                        last = nc.tensor.matmul(out[:, NS * g:NS * g + NS], vn[NG * NS:128, 128 * g:128 * g + 128], wsS[:, g],
                                                start=True, stop=True)
                elif kind == "bt":
                    c = job[1]
                    pe.wait_ge(b_ready, 1)
                    for a in range(4):
                        last = tr(out[:, 128 * a:128 * a + 128], b_nat[:, a, 128 * c:128 * c + 128], ident[:])
                last.then_inc(t_ready, 1)

            def scores(job):
                n = SINDEX[job]
                if n >= 1:
                    pe.wait_ge(s_used, n)
                if job[0] == "piece":
                    j = job[1]
                    g, hd, pair = PIECES[j]
                    if j in (0, 16, 24):
                        pe.wait_ge(t_out, TINDEX[("qk", [u for u in range(60) if UNITS[u][1:3] == ("q", g)][-1])] + 1)
                        pe.wait_ge(const_in, CONSTS)
                    c, r0 = hd // 2, 64 * (hd % 2)
                    mk = bc(masks[:, 2 + g], 1, 4) if g else bc(masks[:, 2:4], 1, 2) if pair else masks[:, 0:4]
                    nc.tensor.matmul(psS[:], identb[:], mk, start=True, stop=False, skip_group_check=True)
                    q_, k_ = qT[g % 2], kT[g % 2]
                    rows = slice(r0, r0 + 64)
                    if g:
                        for a in range(4):
                            last = nc.tensor.matmul(psS[:, 128 * a:128 * a + 128], residue(q_[rows, c], a), residue(k_[rows, c], a),
                                                    start=False, stop=a == 3, skip_group_check=True)
                    else:
                        qv = q_[rows, c].rearrange("p (c i) -> p c i", c=4)
                        kv = k_[rows, c].rearrange("p (c i) -> p c i", c=4)
                        for x in range(2):
                            for y in range(2):
                                b = 2 * pair + x
                                if b - 1 + y < 0:
                                    continue
                                last = nc.tensor.matmul(psS[:, 256 * x + 128 * y:256 * x + 128 * y + 128], qv[:, b], kv[:, b - 1 + y],
                                                        start=False, stop=x == 1 and y == 1, skip_group_check=True)
                elif job[0] == "cache":
                    s = job[1]
                    g, b, r, nt, buf, t0 = KT_AT[s]
                    pe.wait_ge(t_out, TINDEX[("kt", s, nt - 1)] + 1)
                    ov = psS[:, 0:32].rearrange("p (h t) -> p h t", t=4)
                    for x in range(nt):
                        w = {0: 4, 1: 1, 2: 2}[g]
                        for c in range(4):
                            col = T * b + r + x * w
                            last = nc.tensor.matmul(ov[:, 2 * c:2 * c + 2, x * w:x * w + w], KT[:, x, 128 * c:128 * c + 128],
                                                    qb[:, 4 * g + c, :, col:col + w], start=True, stop=True)
                else:
                    for g in ((0, 1) if job[1] == 0 else (2,)):
                        for c in range(4):
                            o = 256 * (g % 2) + 64 * c
                            last = nc.tensor.matmul(psS[0:NS, o:o + 64], kn[:, 4 * g + c], qb[:, 4 * g + c], start=True, stop=True)
                last.then_inc(s_ready, 1)

            def values(j):
                g, hd, pair = PIECES[j]
                pe.wait_ge(t_out, TINDEX[("pt", j)] + 1)
                if j >= 1:
                    pe.wait_ge(o_out, j)
                if j in (0, 16, 24):
                    pe.wait_ge(zeroed, 2)
                W = HD + 1
                if g:
                    for a in range(4):
                        last = nc.tensor.matmul(psO[:, W * a:W * a + W], PT[:, j % 2, 128 * a:128 * a + 128], V[g % 2][:, a, hd],
                                                start=True, stop=True)
                else:
                    for x in range(2):
                        b = 2 * pair + x
                        ys = [y for y in range(2) if b - 1 + y >= 0]
                        for y in ys:
                            o = 256 * x + 128 * y
                            last = nc.tensor.matmul(psO[:, W * x:W * x + W], PT[:, j % 2, o:o + 128], V[0][:, b - 1 + y, hd],
                                                    start=y == ys[0], stop=y == ys[-1])
                last.then_inc(pv_ready, 1)

            def sample_values(q):
                g, b = BUFS[q]
                if q == 0:
                    pe.wait_ge(t_out, TINDEX[("pb", 1)] + 1)
                    for c in range(4):
                        nc.tensor.matmul(psS[:, 64 * c:64 * c + 64], vn[0:NG * NS, 128 * c:128 * c + 128],
                                         Sn[:, 64 * c:64 * c + 64], start=c == 0, stop=False, skip_group_check=True)
                pe.wait_ge(cache_landed[q % 2], landed_count(NBUF + q))
                for x in range(4):
                    if g == 0:
                        col, w = T * (b + x), 4
                    elif g == 1:
                        col, w = T * b + x, 1
                    else:
                        col, w = T * (b + x // 2) + 2 * (x % 2), 2
                    for c in range(4):
                        ov = psS[:, 64 * c:64 * c + 64].rearrange("p (h n) -> p h n", h=2)[:, :, col:col + w]
                        pv = Sc[:, g, 64 * c:64 * c + 64].rearrange("p (h n) -> p h n", h=2)[:, :, col:col + w]
                        last = nc.tensor.matmul(ov, cache[:, q % 2, x, 128 * c:128 * c + 128], pv, start=False,
                                                stop=q == NBUF - 1 and x == 3 and c == 3, skip_group_check=True)
                last.then_inc(cache_used, 1)

            def norm_sum(n):
                pe.wait_ge(ss_done, KD * (n + 1))
                for a in range(4):
                    nc.tensor.matmul(psO[:, a:a + 1], ss[:, 128 * a:128 * a + 128], ones[:, 0:1], start=True, stop=True)
                nc.tensor.matmul(psO[0:NS, 4:5], ss[:, SEQ:NT], ones[:, 0:1], start=True, stop=True).then_inc(n_sum, 1)

            def norm_spread(n):
                pe.wait_ge(n_diag, n + 1)
                nc.tensor.matmul(psS[:], ones[:], sqf[:, 0, 0:SEQ], start=True, stop=True)
                nc.tensor.matmul(psO[:, 0:NS], ones[0:NS, :], sqf[0:NS, 0, SEQ:NT], start=True, stop=True).then_inc(n_sum, 1)

            def y_transposes(m):
                pe.wait_ge(z_used, zc(U_PG + m))
                n = TINDEX[("y", m)]
                pe.wait_ge(t_out, n - 1)
                for a in range(4):
                    nc.tensor.transpose(psT[:, n % 2, 128 * a:128 * a + 128], xT[:, m, 128 * a:128 * a + 128], ident[:])
                if m >= 1:
                    pe.wait_ge(y_nat, m)
                nc.tensor.transpose(psO[0:NS, 0:128], xT[:, m, SEQ:NT], ident[:]).then_inc(t_ready, 1)

            for job in TJOBS[-1]:
                transposes(job)
            pe.wait_ge(h_lo_done, KD)
            for s in range(SLOTS):
                if s == UNIT["wo", 0]:
                    for n in range(len(STEPS[s - 1])):
                        small_step(s - 1, n)
                unit(s)
                if s == UNIT["pj", 3]:
                    norm_sum(0)
                if s == UNIT["pj", 7]:
                    norm_spread(0)
            def hidden_group(j, final=False):
                for q in range(FF_PANELS):
                    pp = j * FF_PANELS + (len(PANELS) + q)
                    pe.wait_ge(w_hi_done, 2 * (pp + 1))
                    pe.wait_ge(w_lo_done, 2 * (pp + 1))
                    for sub in range(2):
                        uu = 2 * q + sub
                        u = j * FF_UNITS + (U_FF + uu)
                        pe.wait_ge(unit_out, u - 1)
                        if q < 4:
                            wk = (lambda k: (h_lo_done, HP + 3 + k + 1)) if uu == 0 else None
                            last = block_unit((P_FF + q) % 2, 256, 128 * sub, KD, uu % 2, h_hi, h_lo, 0, wk)
                        else:
                            wk = (lambda k: (hid_lo, j * KD + (k + 1))) if uu == 8 else None
                            last = block_unit((P_FF + q) % 2, 256, 128 * sub, KD, uu % 2, x2_hi, x2_lo, 0, wk)

            with pe.Fori(0, NFF - 1) as j:
                hidden_group(j)
            hidden_group(NFF - 1, final=True)
            for i in range(4):
                pp = P_PG + i
                pe.wait_ge(w_hi_done, 2 * (pp + 1))
                pe.wait_ge(w_lo_done, 2 * (pp + 1))
                for sub in range(2):
                    u = U_PG + 2 * i + sub
                    m = 2 * i + sub
                    pe.wait_ge(unit_out, u - 1)
                    wk = (lambda k: (h_lo_done, HP + 3 + KD + k + 1)) if m == 0 else None
                    last = block_unit(pp % 2, 256, 128 * sub, KD, u % 2, h_hi, h_lo, 0, wk, u)
                    if m >= 2:
                        y_transposes(m - 2)
            y_transposes(KD - 2)
            y_transposes(KD - 1)

        @block.vector
        def _(dve):
            steps = [0]
            vec = nc.vector

            def link(ins):
                steps[0] += 1
                ins.then_inc(dve_step, 1)
                dve.wait_ge(dve_step, steps[0])

            def split_lo(pp, r):
                for hh in range(2):
                    dve.wait_ge(w_hi_done, pp * 2 + (hh + 1))
                    cols = slice(hh * 1024, hh * 1024 + 1024)
                    vec.tensor_tensor(w_lo[:, r, cols], w_raw[:, hh], w_hi[:, r, cols].bitcast(F32),
                                      ALU.subtract).then_inc(w_lo_done, 1)

            def shape_kq(u):
                sub = UNITS[u][4]
                return (128, 2) if sub < 2 else (NS, 1)

            def sum_squares(u):
                rows, nt = shape_kq(u)
                r, n = (zc(u) - 1) % 2, kqn(u)
                dve.wait_ge(sq_ready, sq_count(u))
                vec.tensor_reduce(st[0:rows, 1, 16 + 8 * (n % 2):16 + 8 * (n % 2) + 4 * nt],
                                  sq[0:rows, r, 0:256 * nt].rearrange("p (h d) -> p h d", d=HD), AX.X, ALU.add).then_inc(ssq_ready, 1)

            def scale_heads(u):
                rows, nt = shape_kq(u)
                r, n = (zc(u) - 1) % 2, kqn(u)
                dve.wait_ge(unit_out, u + 1)
                dve.wait_ge(rstd_ready, n + 1)
                vec.tensor_tensor(sq[0:rows, r, 0:256 * nt].rearrange("p (h d) -> p h d", d=HD),
                                  z[0:rows, r, 0:256 * nt].rearrange("p (h d) -> p h d", d=HD),
                                  bc(st[0:rows, 1, 16 + 8 * (n % 2):16 + 8 * (n % 2) + 4 * nt], 2, HD), ALU.mult).then_inc(z_used, 1)

            def gelu_shape(u):
                kind, sub = UNITS[u][1], UNITS[u][4]
                return (128, NT) if kind == "u" else (128, 512) if sub < 2 else (NS, 256)

            def gelu_inner(u):
                rows, n = gelu_shape(u)
                r = (zc(u) - 1) % 2
                dve.wait_ge(sq_ready, sq_count(u))
                link(vec.tensor_scalar(sq[0:rows, r, 0:n], sq[0:rows, r, 0:n], GELU_A, 1.0, ALU.mult, ALU.add))
                dve.wait_ge(unit_out, u + 1)
                vec.tensor_tensor(sq[0:rows, r, 0:n], sq[0:rows, r, 0:n], z[0:rows, r, 0:n], ALU.mult).then_inc(gelu_arg, 1)

            def gelu_outer(u):
                _, kind, g, i, sub = UNITS[u]
                rows, n = gelu_shape(u)
                r = (zc(u) - 1) % 2
                dve.wait_ge(gelu_tanh, GELU.index(u) + 1)
                if GELU.index(u) == 0:
                    dve.wait_ge(s_ready, SINDEX[("piece", 23)] + 1)
                if kind == "u":
                    dst, th, zz = uT[:, 2 * i + sub], sq[:, r], z[:, r]
                elif sub < 2:
                    dst = va[:, 2 * sub:2 * sub + 2, 256 * i:256 * i + 256]
                    th, zz = (x[:, r, 0:512].rearrange("p (t n) -> p t n", t=2) for x in (sq, z))
                else:
                    dst, th, zz = vn[NG * NS:128, 256 * i:256 * i + 256], sq[0:NS, r, 0:256], z[0:NS, r, 0:256]
                vec.scalar_tensor_tensor(out=dst, in0=th, scalar=1.0, in1=zz, op0=ALU.add, op1=ALU.mult).then_inc(z_used, 1)

            def take_scores(job):
                dve.wait_ge(s_ready, SINDEX[job] + 1)
                if job[0] == "piece":
                    j = job[1]
                    g, hd, pair = PIECES[j]
                    O = (O_blk, O1, O2)[g]
                    if j == 24:
                        dve.wait_ge(o_moved, 256)
                        dve.wait_ge(t_ready, TINDEX[("ws",)] + 1)
                    if j >= 2:
                        dve.wait_ge(t_ready, TINDEX[("pt", j - 2)] + 1)
                    if g:
                        m, sv, pv = O[:, :, hd, 65], psS[:].rearrange("p (a n) -> p a n", a=4), prob[:, j % 2].rearrange("p (a n) -> p a n", a=4)
                        w = 128
                    else:
                        m, sv = O[:, 2 * pair:2 * pair + 2, hd, 65], psS[:].rearrange("p (a n) -> p a n", a=2)
                        pv = prob[:, j % 2].rearrange("p (a n) -> p a n", a=2)
                        w = 256
                    link(vec.tensor_reduce(m, sv, AX.X, ALU.max))
                    vec.tensor_tensor(pv, sv, bc(m, 2, w), ALU.subtract).then_inc(s_used, 1)
                elif job[0] == "cache":
                    g, b, r, nt, buf, t0 = KT_AT[job[1]]
                    w, c0 = {0: (4, T * b), 1: (2, T * b + r), 2: (4, T * b)}[g]
                    vec.tensor_copy(Sc[:, g].rearrange("p (h n) -> p h n", h=H)[:, :, c0:c0 + w],
                                    psS[:, 0:32].rearrange("p (h t) -> p h t", t=4)[:, :, 0:w]).then_inc(s_used, 1)
                elif job[1] == 0:
                    link(vec.tensor_copy(Sn[0:NS], psS[0:NS, 0:256]))
                    vec.tensor_copy(Sn[NS:2 * NS], psS[0:NS, 256:512]).then_inc(s_used, 1)
                else:
                    vec.tensor_copy(Sn[2 * NS:3 * NS], psS[0:NS, 0:256]).then_inc(s_used, 1)

            def take_output(j):
                g, hd, pair = PIECES[j]
                O = (O_blk, O1, O2)[g]
                dve.wait_ge(pv_ready, j + 1)
                W = HD + 1
                if g:
                    dst, n = O[:, :, hd, 0:W], 4
                else:
                    dst, n = O[:, 2 * pair:2 * pair + 2, hd, 0:W], 2
                vec.tensor_copy(dst, psO[:, 0:W * n].rearrange("p (a d) -> p a d", d=W)).then_inc(o_out, 1)

            def flat(O):
                return O[:].rearrange("p a h d -> p (a h) d")

            def add_to_x(m, zslot):
                vec.tensor_tensor(xT[:, m], xT[:, m], z[:, zslot], ALU.add).then_inc(z_used, 1)

            def norm_mean(n):
                dve.wait_ge(n_sum, 2 * n + 1)
                link(vec.tensor_scalar(st[:, 0, 16:20], psO[:, 0:4], 1.0 / D, EPS, ALU.mult, ALU.add))
                vec.tensor_scalar(st[0:NS, 0, 20:21], psO[0:NS, 4:5], 1.0 / D, EPS, ALU.mult, ALU.add).then_inc(n_ms, 1)

            def norm_diagonals(n):
                dve.wait_ge(n_pow, n + 1)
                link(vec.tensor_tensor(sqf[:, 0, 0:SEQ].rearrange("p (a n) -> p a n", a=4), bc(ident[:], 1, 4),
                                       bc(st[:, 0, 16:20], 2, 128), ALU.mult))
                vec.tensor_scalar(sqf[0:NS, 0, SEQ:NT], ident[0:NS, 0:NS], st[0:NS, 0, 20:21], None, ALU.mult).then_inc(n_diag, 1)

            def norm_rows(n):
                dve.wait_ge(n_sum, 2 * n + 2)
                link(vec.tensor_copy(rb[:, 0:SEQ], psS[:]))
                link(vec.tensor_copy(rb[:, SEQ:NT], psO[:, 0:NS]))
                if n == 0:
                    link(vec.tensor_tensor(rb[:], rb[:], rb[:], ALU.mult))

            def gained_lo(n, m):
                dve.wait_ge(h_hi_done, 3 * KD + 3 + n * KD + m + 1)
                vec.scalar_tensor_tensor(out=h_lo[:, m], in0=xT[:, m], scalar=gcol[:, n + 1, m:m + 1], in1=h_hi[:, m].bitcast(F32),
                                         op0=ALU.mult, op1=ALU.subtract).then_inc(h_lo_done, 1)

            def scaled_unit(u, b2, r):
                dve.wait_ge(unit_ready, u + 1)
                vec.tensor_tensor(z[:, r].rearrange("p (n c) -> p n c", n=2), gm[:, 2 * b2:2 * b2 + 2, 0:HALF],
                                  rb[:].rearrange("p (n c) -> p n c", n=2), ALU.mult).then_inc(unit_out, 1)
                dve.wait_ge(unit_out, u + 1)

            dve.wait_ge(x_rstd, 1)
            for a in range(3):
                vec.tensor_scalar(xn[:, a], xn[:, a], st[:, 0, a:a + 1], None, ALU.mult).then_inc(x_scaled, 1)
            for k in range(KD):
                dve.wait_ge(h_hi_done, k + 1)
                vec.scalar_tensor_tensor(out=h_lo[:, k, 0:SEQ], in0=psT[:, k % 2], scalar=gcol[:, 0, k:k + 1],
                                         in1=h_hi[:, k, 0:SEQ].bitcast(F32), op0=ALU.mult, op1=ALU.subtract).then_inc(h_lo_done, 1)
                dve.wait_ge(h_lo_done, k + 1)
            split_lo(0, 0)
            dve.wait_ge(t_ready, TINDEX[("hs",)] + 1)
            v = sq[:, 0, 0:KD * NS].rearrange("p (k n) -> p k n", k=KD)
            vec.tensor_tensor(v, psT[:, 0, 0:KD * NS].rearrange("p (k n) -> p k n", k=KD), bc(gcol[:, 0], 2, NS),
                              ALU.mult).then_inc(t_out, KD + 1)
            dve.wait_ge(h_hi_done, 2 * KD)
            vec.tensor_tensor(h_lo[:, :, SEQ:NT], v, h_hi[:, :, SEQ:NT].bitcast(F32), ALU.subtract).then_inc(h_lo_done, 1)
            for s in range(SLOTS):
                p, kind, g, i, sub = UNITS[s]
                if sub == 0:
                    split_lo(p + 1, (p + 1) % 2)
                if s >= 1 and UNITS[s - 1][1] in ("k", "q"):
                    scale_heads(s - 1)
                if s >= 1 and UNITS[s - 1][1] in ("va", "u"):
                    gelu_outer(s - 1)
                if s == 63:
                    dve.wait_ge(va_rstd, 1)
                    dve.wait_ge(const2_in, CONSTS2)
                    for a in range(4):
                        vec.scalar_tensor_tensor(out=va[:, a], in0=va[:, a], scalar=st[:, 1, a:a + 1], in1=gv_b[:],
                                                 op0=ALU.mult, op1=ALU.mult).then_inc(va_done, 1)
                    vec.scalar_tensor_tensor(out=vas, in0=vas, scalar=st[NG * NS:128, 1, 4:5], in1=gv_b[NG * NS:128],
                                             op0=ALU.mult, op1=ALU.mult).then_inc(va_done, 1)
                if s == 64:
                    dve.wait_ge(o_out, 32)
                    m0, m1, m2 = (flat(O)[:, :, 65] for O in (O0, O1, O2))
                    link(vec.tensor_tensor(mx[:], m0, m1, ALU.max))
                    link(vec.tensor_tensor(mx[:], mx[:], m2, ALU.max))
                    for gg, m in enumerate((m0, m1, m2)):
                        last = vec.tensor_tensor(al[:, gg], m, mx[:], ALU.subtract)
                        if gg < 2:
                            link(last)
                    last.then_inc(al_arg, 1)
                    for hf_ in range(2):
                        dve.wait_ge(t_out, TINDEX[("ss", hf_)] + 1)
                        link(vec.tensor_tensor(smp[hf_][:], smp[hf_][:], smask[:], ALU.add))
                        link(vec.tensor_reduce(st[:, 0, 10 + hf_:11 + hf_], smp[hf_][:], AX.X, ALU.max))
                        vec.tensor_scalar(smp[hf_][:], smp[hf_][:], st[:, 0, 10 + hf_:11 + hf_], None,
                                          ALU.subtract).then_inc(smp_masked, 1)
                if s == 65:
                    for hf_ in range(2):
                        dve.wait_ge(smp_exp, hf_ + 1)
                        link(vec.reciprocal(st[:, 0, 12 + hf_:13 + hf_], st[:, 0, 8 + hf_:9 + hf_]))
                        vec.tensor_scalar(smp[hf_][:], smp[hf_][:], st[:, 0, 12 + hf_:13 + hf_], None,
                                          ALU.mult).then_inc(smp_norm, 1)
                    for gg in range(4):
                        dve.wait_ge(t_out, TINDEX[("mix", gg)] + 1)
                        v = sq[:, gg % 2, 0:SEQ].rearrange("p (c n) -> p c n", c=4)
                        link(vec.tensor_tensor(v, v, bc(bs_b[:, gg], 1, 4), ALU.add))
                        vec.scalar_tensor_tensor(out=uT[:, gg, 0:SEQ], in0=sq[:, gg % 2, 0:SEQ], scalar=0.5, in1=uT[:, gg, 0:SEQ],
                                                 op0=ALU.mult, op1=ALU.mult).then_inc(mix_done, 1)
                    dve.wait_ge(t_out, TINDEX[("mixs",)] + 1)
                    v = sq[:, 0, 0:4 * NS].rearrange("p (g b t) -> p g b t", g=4, b=NB)
                    link(vec.tensor_tensor(v, v, bc(bs_b[:, :, 0:T], 2, NB), ALU.add))
                    vec.scalar_tensor_tensor(out=uT[:, :, SEQ:NT], in0=sq[:, 0, 0:4 * NS].rearrange("p (g n) -> p g n", g=4),
                                             scalar=0.5, in1=uT[:, :, SEQ:NT], op0=ALU.mult, op1=ALU.mult).then_inc(mix_done, 1)
                if s == 66:
                    dve.wait_ge(v_stored[2], V_STORES[2])
                    for gg in range(4):
                        dve.wait_ge(ab_hi, gg + 1)
                        dve.wait_ge(mix_done, 5)
                        vec.tensor_tensor(x2_lo[:, gg], uT[:, gg], x2_hi[:, gg].bitcast(F32), ALU.subtract).then_inc(ab_lo, 1)
                if s == 67:
                    dve.wait_ge(al_exp, 1)
                    dve.wait_ge(o_moved, 256)
                    W = HD + 1
                    o0, o1, o2 = (flat(O)[:, :, 0:W] for O in (O0, O1, O2))
                    link(vec.tensor_tensor(o0, o0, bc(al[:, 0], 2, W), ALU.mult))
                    link(vec.tensor_tensor(o2, o2, bc(al[:, 2], 2, W), ALU.mult))
                    link(vec.tensor_tensor(o0, o0, o2, ALU.add))
                if s == 69:
                    dve.wait_ge(o1_scaled, 1)
                    link(vec.tensor_tensor(o0, o0, o1, ALU.add))
                    link(vec.reciprocal(mx[:], flat(O0)[:, :, HD]))
                    vec.tensor_tensor(b_nat[:].rearrange("p a (h d) -> p (a h) d", d=HD), flat(O0)[:, :, 0:HD], bc(mx[:], 2, HD),
                                      ALU.mult).then_inc(b_ready, 1)
                if s == 72:
                    for c in range(4):
                        dve.wait_ge(t_out, TINDEX[("bt", c)] + 1)
                        vec.tensor_tensor(x2_lo[:, 4 + c, 0:SEQ].rearrange("p (i a) -> p a i", a=4),
                                          sq[:, c % 2, 0:SEQ].rearrange("p (a i) -> p a i", a=4),
                                          x2_hi[:, 4 + c, 0:SEQ].bitcast(F32).rearrange("p (i a) -> p a i", a=4),
                                          ALU.subtract).then_inc(ab_lo, 1)
                if s == V_SLOT0 + NBUF:
                    dve.wait_ge(cache_used, NBUF)
                    dst = sq[:, 0, 0:4 * NS].rearrange("p (c n) -> p c n", c=4)
                    src = psS[:, 0:256].rearrange("p (c h n) -> p c h n", c=4, h=2)
                    link(vec.tensor_copy(dst[0:64], src[0:64, :, 0]))
                    vec.tensor_copy(dst[64:128], src[64:128, :, 1]).then_inc(smp_b, 1)
                if s == V_SLOT0 + NBUF + 1:
                    dve.wait_ge(ab_hi, 9)
                    dve.wait_ge(smp_b, 1)
                    vec.tensor_tensor(x2_lo[:, 4:8, SEQ:NT], sq[:, 0, 0:4 * NS].rearrange("p (c n) -> p c n", c=4),
                                      x2_hi[:, 4:8, SEQ:NT].bitcast(F32), ALU.subtract).then_inc(ab_lo, 1)
                if kind in ("k", "q"):
                    sum_squares(s)
                if kind in ("va", "u"):
                    gelu_inner(s)
                if kind == "oa":
                    m, r = 4 * i + sub, (zc(s) - 1) % 2
                    if m == 0:
                        dve.wait_ge(ab_hi, 4)
                        dve.wait_ge(va_stored, 16 * 2)
                    dve.wait_ge(unit_out, s + 1)
                    vec.scalar_tensor_tensor(out=mA[:, m], in0=tha[:, m % 4], scalar=1.0, in1=z[:, r], op0=ALU.add,
                                             op1=ALU.mult).then_inc(z_used, 1)
                if s - 1 in MERGED:
                    m = MERGED[s - 1]
                    dve.wait_ge(h_hi_done, 2 * KD + m + 1)
                    vec.scalar_tensor_tensor(out=h_lo[:, m], in0=mA[:, m], scalar=0.5, in1=h_hi[:, m].bitcast(F32), op0=ALU.mult,
                                             op1=ALU.subtract).then_inc(h_lo_done, 1)
                if kind == "ob":
                    m, r = 4 * i + sub, (zc(s) - 1) % 2
                    dve.wait_ge(unit_out, s + 1)
                    link(vec.scalar_tensor_tensor(out=z[:, r], in0=thb[:, m], scalar=1.0, in1=z[:, r], op0=ALU.add, op1=ALU.mult))
                    dve.wait_ge(z_used, zc(s) - 1)
                    vec.tensor_tensor(mA[:, m], mA[:, m], z[:, r], ALU.add).then_inc(z_used, 1)
                if kind == "wo":
                    m, r = 2 * i + sub, (zc(s) - 1) % 2
                    if m == 0:
                        dve.wait_ge(t_out, TINDEX[("xs",)] + 1)
                    dve.wait_ge(unit_out, s + 1)
                    add_to_x(m, r)
                if s in (97, 98):
                    k = s - 97
                    dve.wait_ge(t_out, TINDEX[("p", k)] + 1)
                    dve.wait_ge(h_hi_done, 3 * KD + k + 1)
                    vec.tensor_tensor(pT_lo[:, k, 0:SEQ], sqf[:, k, 0:SEQ], pT_hi[:, k, 0:SEQ].bitcast(F32), ALU.subtract).then_inc(h_lo_done, 1)
                if s == 99:
                    dve.wait_ge(t_out, TINDEX[("ps",)] + 1)
                    dve.wait_ge(h_hi_done, 3 * KD + 3)
                    vec.tensor_tensor(pT_lo[:, :, SEQ:NT], sqf[:, 0, 0:2 * NS].rearrange("p (k n) -> p k n", k=2),
                                      pT_hi[:, :, SEQ:NT].bitcast(F32), ALU.subtract).then_inc(h_lo_done, 1)
                if kind == "pj":
                    if sub == 5:
                        norm_mean(0)
                    if sub == 6:
                        norm_diagonals(0)
                    gained_lo(0, sub)
                for job in SJOBS.get(s, []):
                    take_scores(job)
                if s - 2 in S_AT:
                    take_output(S_AT[s - 2])
            norm_rows(0)

            def hidden_group(j, final=False):
                for q in range(FF_PANELS):
                    split_lo(j * FF_PANELS + (P_FF + q + 1), (P_FF + q + 1) % 2)
                    for sub in range(2):
                        uu = 2 * q + sub
                        u = j * FF_UNITS + (U_FF + uu)
                        r = (zc(U_FF) - 1 + uu) % 2
                        if q < 4:
                            dve.wait_ge(unit_out, u + 1)
                            if uu >= 2:
                                dve.wait_ge(hid_lo, j * KD + (uu - 1))
                            vec.tensor_tensor(sqf[:, uu % 2], z[:, r], z[:, r], ALU.mult).then_inc(z_used, 1)
                            dve.wait_ge(z_used, j * FF_UNITS + (zc(U_FF) + uu))
                            dve.wait_ge(hid_hi, j * KD + (uu + 1))
                            vec.tensor_tensor(x2_lo[:, uu], sqf[:, uu % 2], x2_hi[:, uu].bitcast(F32), ALU.subtract).then_inc(hid_lo, 1)
                        else:
                            scaled_unit(u, uu % 2, r)
                            add_to_x(uu - 8, r)
                            if final and uu >= 9:
                                gained_lo(1, uu - 9)

            with dve.Fori(0, NFF - 1) as j:
                hidden_group(j)
            hidden_group(NFF - 1, final=True)
            gained_lo(1, KD - 1)
            split_lo(P_PG + 1, (P_PG + 1) % 2)
            norm_mean(1)
            norm_diagonals(1)
            norm_rows(1)

            def finish_block(m):
                u = U_PG + m
                r = (zc(u) - 1) % 2
                dve.wait_ge(gate_tanh, m + 1)
                link(vec.scalar_tensor_tensor(out=z[:, r], in0=z[:, r], scalar=1.0, in1=proj[:, m], op0=ALU.add, op1=ALU.mult))
                vec.scalar_tensor_tensor(out=xT[:, m], in0=z[:, r], scalar=0.5, in1=xT[:, m], op0=ALU.mult, op1=ALU.add).then_inc(z_used, 1)

            for m in range(KD):
                u = U_PG + m
                if m in (2, 4):
                    split_lo(P_PG + m // 2 + 1, (P_PG + m // 2 + 1) % 2)
                if m >= 2:
                    dve.wait_ge(z_used, zc(u) - 2)
                scaled_unit(u, u % 2, (zc(u) - 1) % 2)
                if m >= 1:
                    finish_block(m - 1)
            finish_block(KD - 1)

        @block.gpsimd
        def _(pool):
            steps = [0]
            gp = nc.gpsimd

            def link(ins):
                steps[0] += 1
                ins.then_inc(pool_step, 1)
                pool.wait_ge(pool_step, steps[0])

            def inverse_root(ap):
                return gp.tensor_tensor(ap, ap, mhalf[0:ap.shape[0], 0:ap.shape[1]], ALU.pow)

            link(gp.memset(mhalf[:], -0.5))
            link(gp.memset(ones[:], 1.0))
            gp.memset(qb[:], 0.0).then_inc(zeroed, 1)
            link(gp.memset(V[0][:, :, :, HD:HD + 1], 1.0))
            gp.memset(V[1][:, :, :, HD:HD + 1], 1.0).then_inc(zeroed, 1)
            pool.wait_ge(x_sq, 5)
            for rows, cols in ((128, slice(0, 4)), (NS, slice(4, 5))):
                v = st[0:rows, 0, cols]
                link(gp.tensor_scalar(v, v, 1.0 / D, EPS, ALU.mult, ALU.add))
                last = inverse_root(v)
                if rows == 128:
                    link(last)
            last.then_inc(x_rstd, 1)
            pool.wait_ge(const_in, CONSTS)

            def copy_window(x):
                n = (WIN[2] - T) * 512 // 4
                pair, part = (x // 4, x % 4) if isinstance(x, int) else x
                src = t["cache2f"][bass.ds(pair, 1), T * 512 + part * n:T * 512 + (part + 1) * n].rearrange("o (x y) -> (o x) y", x=64)
                dst = t["kvs2f"][bass.ds(pair, 1), part * n:(part + 1) * n].rearrange("o (x y) -> (o x) y", x=64)
                pool.dma_start(dst, src).then_inc(cache_copied, 16)

            def finish_heads(u):
                _, qk, g, i, sub = UNITS[u]
                rows, nt = (128, 2) if sub < 2 else (NS, 1)
                n = kqn(u)
                pool.wait_ge(z_used, zc(u))
                if n >= 2:
                    prev = [x for x in range(u) if UNITS[x][1] in ("k", "q") and kqn(x) == n - 2][0]
                    pool.wait_ge(t_ready, TINDEX[("qk", prev)] + 1)
                    if fin_count(n - 2):
                        pool.wait_ge(fin_stored[n % 2], fin_count(n - 2))
                f = fin[0:rows, n % 2, 0:256 * nt]
                r = (zc(u) - 1) % 2
                gain = (gq_b if qk == "q" else gk_b)[0:rows]
                link(gp.tensor_tensor(f.rearrange("p (h d) -> p h d", d=HD), sq[0:rows, r, 0:256 * nt].rearrange("p (h d) -> p h d", d=HD),
                                      bc(gain, 1, 4 * nt), ALU.mult))
                fv = f.rearrange("p (t h d) -> p t h d", t=nt, h=4)
                t0 = 2 * sub if sub < 2 else 4
                cos = bc(cs[0:rows, t0:t0 + nt, 0], 2, 4)
                sn = bc(cs[0:rows, t0:t0 + nt, 1], 2, 4)
                a = rot[0:rows, 0:4 * nt].rearrange("p (t h) d -> p t h d", t=nt)
                b = rot2[0:rows, 0:4 * nt].rearrange("p (t h) d -> p t h d", t=nt)
                link(gp.tensor_tensor(a, fv[:, :, :, 0:16], cos, ALU.mult))
                link(gp.tensor_tensor(b[:, :, :, 0:8], fv[:, :, :, 8:16], sn[:, :, :, 0:8], ALU.mult))
                link(gp.tensor_tensor(b[:, :, :, 8:16], fv[:, :, :, 0:8], sn[:, :, :, 8:16], ALU.mult))
                gp.tensor_tensor(fv[:, :, :, 0:16], a, b, ALU.add).then_inc(fin_ready, 1)

            def add_square(m, n):
                pool.wait_ge(xsq, n + 1)
                if m == 0:
                    if n > 0:
                        pool.wait_ge(n_sum, 1)
                        pool.wait_ge(ss_done, n)
                    gp.tensor_copy(ss[:], sq[:, 0]).then_inc(ss_done, 1)
                else:
                    pool.wait_ge(ss_done, n)
                    gp.tensor_tensor(ss[:], ss[:], sq[:, m % 2], ALU.add).then_inc(ss_done, 1)

            def norm_inverse(n):
                pool.wait_ge(n_ms, n + 1)
                link(inverse_root(st[:, 0, 16:20]))
                inverse_root(st[0:NS, 0, 20:21]).then_inc(n_pow, 1)

            for s in range(SLOTS):
                p, kind, g, i, sub = UNITS[s]
                if s >= 1 and UNITS[s - 1][1] in ("k", "q"):
                    finish_heads(s - 1)
                if kind in ("k", "q"):
                    rows, nt = (128, 2) if sub < 2 else (NS, 1)
                    n = kqn(s)
                    pool.wait_ge(ssq_ready, n + 1)
                    v = st[0:rows, 1, 16 + 8 * (n % 2):16 + 8 * (n % 2) + 4 * nt]
                    link(gp.tensor_scalar(v, v, 1.0 / HD, EPS, ALU.mult, ALU.add))
                    inverse_root(v).then_inc(rstd_ready, 1)
                if s == 37:
                    pool.wait_ge(o_out, 16)
                    for a in range(4):
                        for b in range(4):
                            pool.dma_start(O0[32 * b:32 * b + 32, a], O_blk[a:128:4, b]).then_inc(o_moved, 16)
                if s in COPY_AT:
                    pool.wait_ge(unit_ready, s)
                    copy_window(COPY_AT.index(s))
                if s == 49:
                    pool.wait_ge(const2_in, CONSTS2)
                    pool.wait_ge(fin_ready, kqn(s))
                    gp.tensor_tensor(ws_tril[:], ws_nat[:], bc(tril[:], 1, 4), ALU.mult).then_inc(ws_done, 1)
                if s == 58:
                    pool.wait_ge(ws_rows, 16 * NB)
                    gp.tensor_tensor(wsS.rearrange("p g (b t) -> p g b t", b=NB), bc(wsT4, 2, NB),
                                     bc(same_b.rearrange("p (b t) -> p b t", b=NB), 1, 4), ALU.mult).then_inc(ws_done, 1)
                    pool.wait_ge(ws_done, 2)
                if s == 62:
                    pool.wait_ge(va_sq, 5)
                    for v, half in ((st[:, 1, 0:4], mhalf[:, 0:4]), (st[NG * NS:128, 1, 4:5], mhalf[NG * NS:128, 0:1])):
                        link(gp.tensor_scalar(v, v, 0.25 / DA, EPS, ALU.mult, ALU.add))
                        link(gp.tensor_tensor(v, v, half, ALU.pow))
                        last = gp.tensor_scalar(v, v, 0.5, None, ALU.mult)
                        if v.shape[0] == 128:
                            link(last)
                    last.then_inc(va_rstd, 1)
                    pool.wait_ge(va_rstd, 1)
                if s == 65:
                    pool.wait_ge(al_exp, 1)
                    v = O1[:].rearrange("p a h d -> p (a h) d")[:, :, 0:HD + 1]
                    gp.tensor_tensor(v, v, bc(al[:, 1], 2, HD + 1), ALU.mult).then_inc(o1_scaled, 1)
                if kind == "wo":
                    add_square(2 * i + sub, 2 * i + sub)
            norm_inverse(0)
            def window_parts(j, final=False):
                for q in range(FF_PANELS):
                    pool.wait_ge(unit_ready, j * FF_UNITS + (U_FF + 2 * q))
                    copy_window((j * 2 + (8 + q // 4), q % 4))
                    if final and q >= 4:
                        for m in (2 * (q - 4), 2 * (q - 4) + 1):
                            add_square(m, KD + m)

            with pool.Fori(0, NFF - 1) as j:
                window_parts(j)
            window_parts(NFF - 1, final=True)
            norm_inverse(1)


def constants():
    p = np.arange(128)
    q, k = p[:, None], p[None, :]
    no = np.float32(-1e30)
    zero = np.float32(0)
    before = np.where(k >= q, zero, no)
    never = np.full((128, 128), no)
    causal = np.where(k <= q, zero, no)
    dilated = np.where((k <= q) & ((q - k) % 4 == 0), zero, no)
    masks = np.stack([never, causal, before, causal, dilated], axis=1)
    b, t = np.arange(NS) // T, np.arange(NS) % T
    same = b[:, None] == b[None, :]
    sm, snew = [], []
    for g in range(NG):
        if g == 0:
            old, new = k >= t[:, None], same & (t[None, :] <= t[:, None])
        else:
            old = np.broadcast_to(k >= 0, (NS, 128)) if g == 1 else (k // 64) == (t[:, None] % 2)
            new = same & (t[None, :] == t[:, None])
        sm.append(np.where(old, zero, no))
        snew.append(np.where(new, zero, no))
    smask = np.tile(np.concatenate(sm + snew, axis=1), (4, 1)).astype(np.float32)
    half = HD // 8
    inv = (np.float32(500000.0) ** (-np.arange(half, dtype=np.float32) * np.float32(2.0) / np.float32(2 * half))).astype(np.float32)
    rot = np.zeros((128, 5, 2, 16), np.float32)
    for a in range(5):
        rows = np.arange(128 if a < 4 else NS)
        pos = (128 * a + rows if a < 4 else WIN[2] + rows % T).astype(np.float32)
        ang = (pos[:, None] * inv[None, :]).astype(np.float32)
        c, s = np.cos(ang), np.sin(ang)
        rot[:len(rows), a, 0] = np.concatenate([c, c], axis=1)
        rot[:len(rows), a, 1] = np.concatenate([-s, s], axis=1)

    def bf16_bits(a):
        return (np.ascontiguousarray(a, dtype=np.float32).view(np.uint32) >> 16).astype(np.uint16)

    return {"c_ident": np.eye(128, dtype=np.float32), "c_identb": bf16_bits(np.eye(128)), "c_masks": bf16_bits(masks),
            "c_rot": rot, "c_tril": (k <= q).astype(np.float32), "c_smask": smask,
            "c_same": (same & (t[:, None] <= t[None, :])).astype(np.float32)}


_OUTS = [("y_prompt", (1, SEQ, D)), ("y_sample", (NB, T, D))] + \
    [(f"kvp{g}", (1, 1, 2, min(WIN[g], SEQ), H, HD)) for g in range(NG)] + \
    [(f"kvs{g}", (1, NB, 2, WIN[g], H, HD)) for g in range(NG)] + \
    [("cvp", (1, 1, 128, DA)), ("cvs", (1, NB, T, DA))]


def kernel(**inputs):
    import concourse.bacc as bacc
    from concourse.bass_utils import run_bass_kernel_spmd

    nc = bacc.Bacc("TRN2", target_bir_lowering=False, num_devices=1)
    arrays, ap = {}, {}
    for name, value in list(inputs.items()) + list(constants().items()):
        a = np.ascontiguousarray(value)
        arrays[f"in_{name}"] = a
        ap[name] = nc.dram_tensor(f"in_{name}", a.shape, mybir.dt.from_np(a.dtype), kind="ExternalInput").ap()
    for name, shape in _OUTS:
        ap[name] = nc.dram_tensor(f"out_{name}", shape, F32, kind="ExternalOutput").ap()
    t = dict(ap)
    for name in inputs:
        if name not in ("x_prompt", "x_sample"):
            t[name] = ap[name][0]
    for name in ("c_identb", "c_masks"):
        t[name] = ap[name].bitcast(BF16)
    t["x_prompt"] = ap["x_prompt"][0]
    t["x_sample"] = ap["x_sample"].rearrange("b t d -> (b t) d")
    t["p_prompt"] = ap["p_prompt"][0, 0]
    t["p_sample"] = ap["p_sample"][0].rearrange("b t d -> (b t) d")
    t["y_prompt"] = ap["y_prompt"][0]
    t["y_sample"] = ap["y_sample"].rearrange("b t d -> (b t) d")
    for g, name in enumerate(("cache_kv_w128", "cache_kv_w512", "cache_kv_w2048")):
        t[f"cache{g}"] = ap[name][0].rearrange("b v w h d -> b v w (h d)")
        t[f"kvp{g}"] = ap[f"kvp{g}"][0, 0].rearrange("v w h d -> v w (h d)")
        t[f"kvs{g}"] = ap[f"kvs{g}"][0].rearrange("b v w h d -> b v w (h d)")
    t["cache2f"] = ap["cache_kv_w2048"][0].rearrange("b v w h d -> (b v) (w h d)")
    t["kvs2f"] = ap["kvs2"][0].rearrange("b v w h d -> (b v) (w h d)")
    t["cvp"] = ap["cvp"][0, 0]
    t["cvs"] = ap["cvs"][0].rearrange("b t d -> (b t) d")
    build(nc, t)
    r = run_bass_kernel_spmd(nc, [arrays], core_ids=[0])
    return tuple(r.results[0][f"out_{name}"] for name, _ in _OUTS)
```
